# Optimizing a Trainium2 kernel written in Bass

```python
import math
import jax, jax.numpy as jnp
from jax import lax
import numpy as np

D_MODEL = 2048
BATCH = 1
SEQ = 256
DEPTH = 2
DEC_BATCH = 1
DEC_SEQ = 64
PAST_LEN = 512

CHUNK = 64
QBLOCK = 128
HEAD_DIM = 64
MIX_WIDTH = D_MODEL
GROUP_WIDTH = MIX_WIDTH // 4
A_HEADS = GROUP_WIDTH // HEAD_DIM
A_KV_HEADS = 2
A_WINDOW = 128
A_WIN_CHUNKS = A_WINDOW // CHUNK
B_HEADS = 4
B_QK_DIM = 64
B_V_DIM = GROUP_WIDTH // B_HEADS
C_HEADS = 8
C_Q_RANK = 384
C_KV_RANK = 128
C_NOPE = 64
C_ROPE = 32
C_V_DIM = GROUP_WIDTH // C_HEADS
ROPE_THETA = 10000.0
D_HEADS = 8
D_HEAD_DIM = GROUP_WIDTH // D_HEADS
D_FF = 4 * D_MODEL
PLE_DIM = 256
NORM_EPS = 1e-6
NEG = -1e30

IN_SPLITS = (A_HEADS * HEAD_DIM, A_KV_HEADS * HEAD_DIM, A_KV_HEADS * HEAD_DIM,
             B_HEADS * 2 * B_QK_DIM, B_HEADS * 2 * B_QK_DIM, B_HEADS * B_V_DIM,
             C_Q_RANK, C_KV_RANK, C_ROPE,
             D_HEADS * D_HEAD_DIM, D_HEADS * D_HEAD_DIM, D_HEADS * D_HEAD_DIM, D_HEADS)
IN_WIDTH = sum(IN_SPLITS)

kernel_name = 'hybrid_stream_encoder_step'

def rms_norm(x, g):
    xf = x.astype(jnp.float32)
    y = xf * lax.rsqrt(jnp.mean(xf * xf, axis=-1, keepdims=True) + NORM_EPS)
    return (y * g.astype(jnp.float32)).astype(x.dtype)

def alibi_slopes(n):
    return jnp.asarray(2.0 ** (-8.0 * np.arange(1, n + 1) / n), dtype=jnp.float32)

def apply_rope(x, pos):
    half = x.shape[-1] // 2
    inv = ROPE_THETA ** (-jnp.arange(half, dtype=jnp.float32) / half)
    ang = pos.astype(jnp.float32)[:, None] * inv
    ang = ang.reshape(ang.shape[0], *([1] * (x.ndim - 3)), half)
    cos, sin = jnp.cos(ang), jnp.sin(ang)
    x1 = x[..., :half].astype(jnp.float32)
    x2 = x[..., half:].astype(jnp.float32)
    return jnp.concatenate([x1 * cos - x2 * sin, x2 * cos + x1 * sin], axis=-1).astype(x.dtype)

def map_query_blocks(fn, *arrays):
    t = arrays[0].shape[1]
    if t <= QBLOCK or t % QBLOCK:
        return fn(*arrays)
    nb = t // QBLOCK
    def split(a):
        return jnp.moveaxis(a.reshape(a.shape[0], nb, QBLOCK, *a.shape[2:]), 1, 0)
    out = lax.map(lambda args: fn(*args), tuple(split(a) for a in arrays))
    out = jnp.moveaxis(out, 0, 1)
    return out.reshape(out.shape[0], t, *out.shape[3:])

def window_attention(q, k, v, qpos, kpos, sinks, slopes):
    b, n, tq, h, d = q.shape
    kvh = k.shape[3]
    r = h // kvh
    qg = q.reshape(b, n, tq, kvh, r, d)
    s = jnp.einsum('bnqgrd,bnkgd->bngrqk', qg, k, preferred_element_type=jnp.float32) * (1.0 / math.sqrt(d))
    qc = (qpos // CHUNK)[:, :, None]
    kc = (kpos // CHUNK)[:, None, :]
    valid = (kpos[:, None, :] >= 0) & (kc <= qc) & (kc >= qc - A_WIN_CHUNKS)
    dist = jnp.abs(qpos[:, :, None] - kpos[:, None, :]).astype(jnp.float32)
    bias = -slopes.reshape(kvh, r)[None, :, :, None, None] * dist[:, None, None]
    s = jnp.where(valid[:, None, None], s + bias, NEG)
    sink = sinks.astype(jnp.float32).reshape(kvh, r, 1, 1)
    m = jnp.maximum(s.max(axis=-1, keepdims=True), sink)
    p = jnp.exp(s - m)
    p = p / (p.sum(axis=-1, keepdims=True) + jnp.exp(sink - m))
    o = jnp.einsum('bngrqk,bnkgd->bnqgrd', p.astype(v.dtype), v)
    return o.reshape(b, n * tq, h * d)

def diff_attention(q, k, v, qpos, kpos, lam, slopes):
    d = q.shape[-1]
    def block(qb, qpb):
        qp = qpb[0]
        s = jnp.einsum('bqhcd,bkhcd->bhcqk', qb, k, preferred_element_type=jnp.float32) * (1.0 / math.sqrt(d))
        valid = (kpos[None, :] // CHUNK) <= (qp[:, None] // CHUNK)
        dist = jnp.abs(qp[:, None] - kpos[None, :]).astype(jnp.float32)
        s = jnp.where(valid, s - slopes[:, None, None, None] * dist, NEG)
        a = jax.nn.softmax(s, axis=-1)
        w = a[:, :, 0] - lam * a[:, :, 1]
        return jnp.einsum('bhqk,bkhe->bqhe', w.astype(v.dtype), v)
    return map_query_blocks(block, q, qpos)

def mla_attention(q_nope, q_rope, k_nope, k_rope, v, qpos, kpos):
    scale = 1.0 / math.sqrt(q_nope.shape[-1] + q_rope.shape[-1])
    def block(qn, qr, qpb):
        qp = qpb[0]
        s = (jnp.einsum('bqhd,bkhd->bhqk', qn, k_nope, preferred_element_type=jnp.float32)
             + jnp.einsum('bqhd,bkd->bhqk', qr, k_rope, preferred_element_type=jnp.float32)) * scale
        valid = (kpos[None, :] // CHUNK) <= (qp[:, None] // CHUNK)
        a = jax.nn.softmax(jnp.where(valid, s, NEG), axis=-1)
        return jnp.einsum('bhqk,bkhe->bqhe', a.astype(v.dtype), v)
    return map_query_blocks(block, q_nope, q_rope, qpos)

def forgetting_attention(q, k, v, fq, fk, qpos, kpos):
    d = q.shape[-1]
    fk_t = jnp.moveaxis(fk, 1, 2)[:, :, None, :]
    def block(qb, fqb, qpb):
        qp = qpb[0]
        s = jnp.einsum('bqhd,bkhd->bhqk', qb, k, preferred_element_type=jnp.float32) * (1.0 / math.sqrt(d))
        s = s + (jnp.moveaxis(fqb, 1, 2)[:, :, :, None] - fk_t)
        valid = kpos[None, :] <= qp[:, None]
        a = jax.nn.softmax(jnp.where(valid, s, NEG), axis=-1)
        return jnp.einsum('bhqk,bkhe->bqhe', a.astype(v.dtype), v)
    return map_query_blocks(block, q, fq, qpos)

def trunk_layer(x, ple, past, li,
                g_mix, w_in, a_gq, a_gk, a_sinks,
                b_gq, b_gk, b_lq1, b_lk1, b_lq2, b_lk2, b_gout,
                c_gcq, c_wq_up, c_gckv, c_wkv_up, c_gqn, c_gkn, c_gqr, c_gkr,
                d_gq, d_gk, d_bf, w_out, g_mlp, w_up, w_down, g_ple, w_ple, w_ple_gate):
    bsz, t, _ = x.shape
    p_len = 0 if past is None else past[2].shape[1]
    qpos = p_len + jnp.arange(t)
    kpos = jnp.arange(p_len + t)

    h = rms_norm(x, g_mix)
    offs = np.cumsum(IN_SPLITS)[:-1].tolist()
    (aq, ak, av, bq, bk, bv, ccq, cckv, ckr, dq, dk, dv, dfl) = jnp.split(h @ w_in, offs, axis=-1)

    def with_past(i, new):
        return new if past is None else jnp.concatenate([past[i].astype(new.dtype), new], axis=1)

    aq = rms_norm(aq.reshape(bsz, t, A_HEADS, HEAD_DIM), a_gq)
    ak = rms_norm(ak.reshape(bsz, t, A_KV_HEADS, HEAD_DIM), a_gk)
    av = av.reshape(bsz, t, A_KV_HEADS, HEAD_DIM)
    slopes_a = alibi_slopes(A_HEADS)
    if past is None:
        nc = t // CHUNK
        wc = A_WIN_CHUNKS
        def band(z):
            zc = z.reshape(bsz, nc, CHUNK, *z.shape[2:])
            zp = jnp.pad(zc, ((0, 0), (wc, 0)) + ((0, 0),) * (zc.ndim - 2))
            return jnp.concatenate([zp[:, j:j + nc] for j in range(wc + 1)], axis=2)
        qp_a = jnp.arange(nc)[:, None] * CHUNK + jnp.arange(CHUNK)[None]
        kp_a = (jnp.arange(nc)[:, None] - wc) * CHUNK + jnp.arange((wc + 1) * CHUNK)[None]
        oa = window_attention(aq.reshape(bsz, nc, CHUNK, A_HEADS, HEAD_DIM), band(ak), band(av),
                              qp_a, kp_a, a_sinks, slopes_a)
        keep = min(A_WINDOW, t)
        new_ak, new_av = ak[:, t - keep:], av[:, t - keep:]
    else:
        lc = past[0].shape[1]
        k_all = jnp.concatenate([past[0].astype(ak.dtype), ak], axis=1)
        v_all = jnp.concatenate([past[1].astype(av.dtype), av], axis=1)
        kp_a = jnp.concatenate([p_len - lc + jnp.arange(lc), qpos])[None]
        oa = window_attention(aq[:, None], k_all[:, None], v_all[:, None], qpos[None], kp_a, a_sinks, slopes_a)
        new_ak, new_av = k_all[:, -lc:], v_all[:, -lc:]

    bq = rms_norm(bq.reshape(bsz, t, B_HEADS, 2, B_QK_DIM), b_gq)
    bk = rms_norm(bk.reshape(bsz, t, B_HEADS, 2, B_QK_DIM), b_gk)
    bv = bv.reshape(bsz, t, B_HEADS, B_V_DIM)
    lam_init = 0.8 - 0.6 * math.exp(-0.3 * li)
    lam = (jnp.exp(jnp.sum(b_lq1.astype(jnp.float32) * b_lk1.astype(jnp.float32)))
           - jnp.exp(jnp.sum(b_lq2.astype(jnp.float32) * b_lk2.astype(jnp.float32))) + lam_init)
    ob = diff_attention(bq, with_past(2, bk), with_past(3, bv), qpos[None], kpos, lam, alibi_slopes(B_HEADS))
    ob = (rms_norm(ob, b_gout) * (1.0 - lam_init)).reshape(bsz, t, GROUP_WIDTH)

    cq = (rms_norm(ccq, c_gcq) @ c_wq_up).reshape(bsz, t, C_HEADS, C_NOPE + C_ROPE)
    q_nope = rms_norm(cq[..., :C_NOPE], c_gqn)
    q_rope = apply_rope(rms_norm(cq[..., C_NOPE:], c_gqr), qpos)
    ckv = rms_norm(cckv, c_gckv)
    kr = apply_rope(rms_norm(ckr, c_gkr), qpos)
    ckv_all = with_past(4, ckv)
    kr_all = with_past(5, kr)
    kv = (ckv_all @ c_wkv_up).reshape(bsz, p_len + t, C_HEADS, C_NOPE + C_V_DIM)
    k_nope = rms_norm(kv[..., :C_NOPE], c_gkn)
    oc = mla_attention(q_nope, q_rope, k_nope, kr_all, kv[..., C_NOPE:], qpos[None], kpos)
    oc = oc.reshape(bsz, t, GROUP_WIDTH)

    dq = rms_norm(dq.reshape(bsz, t, D_HEADS, D_HEAD_DIM), d_gq)
    dk = rms_norm(dk.reshape(bsz, t, D_HEADS, D_HEAD_DIM), d_gk)
    dv = dv.reshape(bsz, t, D_HEADS, D_HEAD_DIM)
    logf = jax.nn.log_sigmoid(dfl.astype(jnp.float32) + d_bf.astype(jnp.float32))
    logf_all = logf if past is None else jnp.concatenate([past[8].astype(jnp.float32), logf], axis=1)
    cum_f = jnp.cumsum(logf_all, axis=1)
    od = forgetting_attention(dq, with_past(6, dk), with_past(7, dv), cum_f[:, p_len:], cum_f, qpos[None], kpos)
    od = od.reshape(bsz, t, GROUP_WIDTH)

    x = x + jnp.concatenate([oa, ob, oc, od], axis=-1) @ w_out
    x = x + jnp.square(jax.nn.relu(rms_norm(x, g_mlp) @ w_up)) @ w_down
    x = x + (ple.astype(x.dtype) @ w_ple) * jax.nn.sigmoid(rms_norm(x, g_ple) @ w_ple_gate)
    return x, (new_ak, new_av, bk, bv, ckv, kr, dk, dv, logf)

def setup_inputs(seed: int = 0) -> dict:
    key = jax.random.key(seed)
    ks = iter(jax.random.split(key, 64))
    def nrm(shape, scale=1.0):
        return jax.random.normal(next(ks), shape, jnp.float32) * scale
    def gain(n):
        return 1.0 + 0.02 * nrm((DEPTH, n))
    a_buf = min(A_WINDOW, PAST_LEN)
    return {
        'x_prompt': nrm((BATCH, SEQ, D_MODEL)),
        'x_sample': nrm((DEC_BATCH, DEC_SEQ, D_MODEL)),
        'p_prompt': nrm((DEPTH, BATCH, SEQ, PLE_DIM)),
        'p_sample': nrm((DEPTH, DEC_BATCH, DEC_SEQ, PLE_DIM)),
        'cache_a_k': nrm((DEPTH, DEC_BATCH, a_buf, A_KV_HEADS, HEAD_DIM)),
        'cache_a_v': nrm((DEPTH, DEC_BATCH, a_buf, A_KV_HEADS, HEAD_DIM)),
        'cache_b_k': nrm((DEPTH, DEC_BATCH, PAST_LEN, B_HEADS, 2, B_QK_DIM)),
        'cache_b_v': nrm((DEPTH, DEC_BATCH, PAST_LEN, B_HEADS, B_V_DIM)),
        'cache_c_kv': nrm((DEPTH, DEC_BATCH, PAST_LEN, C_KV_RANK)),
        'cache_c_krope': nrm((DEPTH, DEC_BATCH, PAST_LEN, C_ROPE)),
        'cache_d_k': nrm((DEPTH, DEC_BATCH, PAST_LEN, D_HEADS, D_HEAD_DIM)),
        'cache_d_v': nrm((DEPTH, DEC_BATCH, PAST_LEN, D_HEADS, D_HEAD_DIM)),
        'cache_d_logf': jax.nn.log_sigmoid(nrm((DEPTH, DEC_BATCH, PAST_LEN, D_HEADS)) + 2.0),
        'g_mix': gain(D_MODEL),
        'w_in': nrm((DEPTH, D_MODEL, IN_WIDTH), D_MODEL ** -0.5),
        'a_gq': gain(HEAD_DIM),
        'a_gk': gain(HEAD_DIM),
        'a_sinks': nrm((DEPTH, A_HEADS), 0.5),
        'b_gq': gain(B_QK_DIM),
        'b_gk': gain(B_QK_DIM),
        'b_lq1': nrm((DEPTH, B_QK_DIM), 0.1),
        'b_lk1': nrm((DEPTH, B_QK_DIM), 0.1),
        'b_lq2': nrm((DEPTH, B_QK_DIM), 0.1),
        'b_lk2': nrm((DEPTH, B_QK_DIM), 0.1),
        'b_gout': gain(B_V_DIM),
        'c_gcq': gain(C_Q_RANK),
        'c_wq_up': nrm((DEPTH, C_Q_RANK, C_HEADS * (C_NOPE + C_ROPE)), C_Q_RANK ** -0.5),
        'c_gckv': gain(C_KV_RANK),
        'c_wkv_up': nrm((DEPTH, C_KV_RANK, C_HEADS * (C_NOPE + C_V_DIM)), C_KV_RANK ** -0.5),
        'c_gqn': gain(C_NOPE),
        'c_gkn': gain(C_NOPE),
        'c_gqr': gain(C_ROPE),
        'c_gkr': gain(C_ROPE),
        'd_gq': gain(D_HEAD_DIM),
        'd_gk': gain(D_HEAD_DIM),
        'd_bf': 2.0 + 0.1 * nrm((DEPTH, D_HEADS)),
        'w_out': nrm((DEPTH, MIX_WIDTH, D_MODEL), MIX_WIDTH ** -0.5),
        'g_mlp': gain(D_MODEL),
        'w_up': nrm((DEPTH, D_MODEL, D_FF), D_MODEL ** -0.5),
        'w_down': nrm((DEPTH, D_FF, D_MODEL), 0.7 * D_FF ** -0.5),
        'g_ple': gain(D_MODEL),
        'w_ple': nrm((DEPTH, PLE_DIM, D_MODEL), PLE_DIM ** -0.5),
        'w_ple_gate': nrm((DEPTH, D_MODEL, D_MODEL), D_MODEL ** -0.5),
    }

def reference(x_prompt, x_sample, p_prompt, p_sample,
              cache_a_k, cache_a_v, cache_b_k, cache_b_v, cache_c_kv, cache_c_krope,
              cache_d_k, cache_d_v, cache_d_logf,
              g_mix, w_in, a_gq, a_gk, a_sinks,
              b_gq, b_gk, b_lq1, b_lk1, b_lq2, b_lk2, b_gout,
              c_gcq, c_wq_up, c_gckv, c_wkv_up, c_gqn, c_gkn, c_gqr, c_gkr,
              d_gq, d_gk, d_bf, w_out, g_mlp, w_up, w_down, g_ple, w_ple, w_ple_gate):
    weights = (g_mix, w_in, a_gq, a_gk, a_sinks,
               b_gq, b_gk, b_lq1, b_lk1, b_lq2, b_lk2, b_gout,
               c_gcq, c_wq_up, c_gckv, c_wkv_up, c_gqn, c_gkn, c_gqr, c_gkr,
               d_gq, d_gk, d_bf, w_out, g_mlp, w_up, w_down, g_ple, w_ple, w_ple_gate)
    caches = (cache_a_k, cache_a_v, cache_b_k, cache_b_v, cache_c_kv, cache_c_krope,
              cache_d_k, cache_d_v, cache_d_logf)
    yp, ys = x_prompt, x_sample
    st_p = [[] for _ in caches]
    st_s = [[] for _ in caches]
    for li in range(DEPTH):
        lw = [w[li] for w in weights]
        yp, new_p = trunk_layer(yp, p_prompt[li], None, li, *lw)
        ys, new_s = trunk_layer(ys, p_sample[li], tuple(c[li] for c in caches), li, *lw)
        for lst, s in zip(st_p, new_p):
            lst.append(s)
        for lst, s in zip(st_s, new_s):
            lst.append(s)
    (a_k_p, a_v_p, b_k_p, b_v_p, c_kv_p, c_krope_p, d_k_p, d_v_p, d_logf_p) = [jnp.stack(l) for l in st_p]
    (a_k_s, a_v_s, b_k_s, b_v_s, c_kv_s, c_krope_s, d_k_s, d_v_s, d_logf_s) = [jnp.stack(l) for l in st_s]
    return (yp, ys,
            a_k_p, a_v_p, b_k_p, b_v_p, c_kv_p, c_krope_p, d_k_p, d_v_p, d_logf_p,
            a_k_s, a_v_s, b_k_s, b_v_s, c_kv_s, c_krope_s, d_k_s, d_v_s, d_logf_s)


_drawn_inputs = setup_inputs


def setup_inputs(seed=0):
    import zlib

    import numpy as np

    out = dict(_drawn_inputs(seed))
    spreads = {}
    factors = {'cache_c_krope': 2.976,
     'cache_d_logf': 46.521,
     'a_gq': 8.0,
     'a_gk': 2.739,
     'a_sinks': 64.0,
     'b_gq': 7.662,
     'b_gk': 2.847,
     'b_lq1': 3.93,
     'b_gout': 6.09,
     'c_gcq': 8.0,
     'c_gckv': 2.794,
     'c_gqn': 8.0,
     'c_gkn': 8.0,
     'c_gqr': 8.0,
     'c_gkr': 2.929,
     'd_gq': 8.0,
     'd_gk': 2.948,
     'g_mlp': 3.199,
     'g_ple': 200.0}
    for name, (base, spread) in spreads.items():
        noise = np.random.default_rng([zlib.crc32(name.encode()), seed]).standard_normal(out[name].shape)
        drawn = base * np.exp(spread * noise) if base else spread * noise
        out[name] = __import__('jax').numpy.asarray(drawn.astype(out[name].dtype))
    for name, factor in factors.items():
        out[name] = (out[name] * factor).astype(out[name].dtype)
    return out
```

```python
import concourse.bass as bass
from concourse import mybir
from contextlib import ExitStack

DM, SEQ, DSEQ, PAST, DEPTH = 2048, 256, 64, 512, 2
TOK = SEQ + DSEQ
CHUNK, WINDOW = 64, 128
HD = 64
ROPE, CQR, CKVR = 32, 384, 128
FF, PLE = 8192, 256
EPS = 1e-6
NEG = -1e30
KB = DM // 128
UK = 2
RING = 4
FG = FF // DM
W_A, W_B, W_CL, W_CR, W_D, W_F = 0, 768, 2304, 2816, 2848, 4384
CEXT, DEXT = HD + ROPE, HD + 2
KEYS = PAST + DSEQ
ALLK = KEYS + SEQ

T_ID, T_TRI, T_NDA, T_NDB, T_MC, T_MD, T_NDS, T_COS, T_SIN, T_END = (
    0, 128, 256, 512, 768, 896, 1024, 1600, 1648, 1696)

VECS = [("a_gq", HD), ("a_gk", HD), ("b_gq", HD), ("b_gk", HD), ("d_gq", HD), ("d_gk", HD), ("c_gcq", CQR),
        ("c_gckv", CKVR), ("c_gkr", ROPE), ("c_gqn", HD), ("c_gqr", ROPE), ("c_gkn", HD), ("b_gout", 128),
        ("a_sinks", 8), ("d_bf", 8), ("b_lq1", HD), ("b_lk1", HD), ("b_lq2", HD), ("b_lk2", HD), ("lam_init", 2)]
VOFF, _n = {}, 0
for _name, _w in VECS:
    VOFF[_name] = _n
    _n += _w
VW = _n

GROUPS = "AABBCCDD"
MAPS = 4


def items_of(group):
    return [((0, 1), 0, 128), ((2, 3), 128, 128)] if group == "B" else [((m,), m * HD, HD) for m in range(MAPS)]


ITEMS = [(j, maps, col, w) for j, g in enumerate(GROUPS) for maps, col, w in items_of(g)]
N_ITEMS = len(ITEMS)
N_MAPS = MAPS * len(GROUPS)


def build(nc, I, O):
    f32 = mybir.dt.float32
    ALU, ACT, AX = mybir.AluOpType, mybir.ActivationFunctionType, mybir.AxisListType
    X = AX.X
    ctx = ExitStack()
    with ctx:
        f32r = mybir.dt.float32r
        top = [nc.sbuf_base + (-nc.sbuf_base) % 64]

        def sb(name, shape, dtype=f32, at=None):
            words = 1
            for n in shape[1:]:
                words *= n
            if at is None:
                at = top[0]
                top[0] += 4 * (words + (-words) % 8)
            return nc.alloc_sbuf_tensor_at(name, shape, dtype, offset=at)

        def sem(name):
            return ctx.enter_context(nc.semaphore(name))

        x = sb("x", [128, KB, TOK])
        at = top[0]
        xg = sb("xg", [128, KB * TOK + 64])
        xhi = sb("xhi", [128, KB, TOK], f32r, at)
        at = top[0]
        hid = sb("hid", [128, KB, TOK])
        hhi = sb("hhi", [128, KB, TOK], f32r, at)
        ring = sb("ring", [128, RING, 1024])
        table = sb("table", [128, T_END])
        vec = sb("vec", [128, VW])
        gains = sb("gains", [128, 3, KB])
        ones = sb("ones", [128, 128])
        eps = sb("eps", [128, 1])
        arena = sb("arena", [128, KB * TOK])
        proj = arena[:, 0:3 * 1544].rearrange("p (t n) -> p t n", t=3)
        plout = arena[:, :].rearrange("p (b n) -> p b n", b=KB)
        otok = sb("otok", [128, 3, 256])
        otmp = sb("otmp", [128, 3, 256])
        flog = sb("flog", [128, 7, 8])
        fcum = sb("fcum", [128, 7, 8])
        fsm = sb("fsm", [128, 8, 24])
        mx = sb("mx", [128, N_MAPS, 3])
        sums = sb("sums", [128, N_MAPS, 3])
        sm = sb("sm", [128, N_MAPS, 3])
        es = sb("es", [128, 8, 3])
        rinv = sb("rinv", [128, N_MAPS, 3])
        ssq = sb("ssq", [128, 64])
        root = sb("root", [128, 64])
        rstd = sb("rstd", [128, 64])
        lam = sb("lam", [128, 8])
        rtok = sb("rtok", [128, 3])
        rroot = sb("rroot", [128, TOK])
        rfeat = sb("rfeat", [128, TOK])
        acc = sb("acc", [128, TOK + 64])
        t0 = sb("t0", [128, 2, TOK])
        t1 = sb("t1", [128, 2, TOK])
        pleh = sb("pleh", [128, 2, TOK], f32r)
        plel = sb("plel", [128, 2, TOK], f32r)
        region = top[0]
        cqT = sb("cqT", [128, 3 * TOK + 64])
        ckvT = sb("ckvT", [128, ALLK])
        kT = sb("kT", [128, MAPS, ALLK])
        qT = sb("qT", [128, MAPS, TOK])
        kext = sb("kext", [128, 7, MAPS, CEXT])
        qext = sb("qext", [128, 3, MAPS, CEXT])
        vtok = sb("vtok", [128, 7, 256])
        kcache = sb("kcache", [128, 4, 256])
        prob = sb("prob", [128, 4, 960])
        probT = sb("probT", [128, 704])
        end, top[0] = top[0], region
        cqT_pad = cqT[:, 3 * TOK:]
        whi = sb("whi", [128, RING, 1024], f32r)
        wlo = sb("wlo", [128, RING, 1024], f32r)
        at = top[0]
        xlo = sb("xlo", [128, KB, TOK], f32r)
        htmp = sb("htmp", [128, 2, 4, TOK], f32r, at)
        hlo = sb("hlo", [128, KB, TOK], f32r)
        assert max(end, top[0]) <= nc.sbuf_usable_end
        sq = prob[:, :, :].rearrange("p a b -> p (a b)")
        ps = ctx.enter_context(nc.psum_tensor("ps", [128, 8, 512], f32))
        psf = ps[:, :, :].rearrange("p b n -> p (b n)")

        ident = table[:, T_ID:T_ID + 128]
        tri = table[:, T_TRI:T_TRI + 128]
        cos = table[:, T_COS:T_COS + 48].rearrange("p (t n) -> p t n", t=3)
        sin = table[:, T_SIN:T_SIN + 48].rearrange("p (t n) -> p t n", t=3)

        def v(name):
            w = dict(VECS)[name]
            return vec[:, VOFF[name]:VOFF[name] + w]


        raw_loaded = [sem(f"raw_loaded{i}") for i in range(RING)]
        unit_used = sem("unit_used")
        bank_full = sem("bank_full")
        half_free = sem("half_free")
        hid_ready = sem("hid_ready")
        gained = sem("gained")
        split_ready = sem("split_ready")
        hi_ready = sem("hi_ready")
        lo_ready = sem("lo_ready")
        acc_ready = sem("acc_ready")
        rms_summed = sem("rms_summed")
        rms_ready = sem("rms_ready")
        inv_ready = sem("inv_ready")
        sig_in = sem("sig_in")
        sig_ready = sem("sig_ready")
        proj_full = sem("proj_full")
        proj_copied = sem("proj_copied")
        sq_ready = sem("sq_ready")
        ssq_ready = sem("ssq_ready")
        root_ready = sem("root_ready")
        group_ready = sem("group_ready")
        prep_full = sem("prep_full")
        prep_copied = [sem("prep_copied_act"), sem("prep_copied_dve")]
        ext_ready = sem("ext_ready")
        lat_full = sem("lat_full")
        lat_copied = [sem("lat_copied_act"), sem("lat_copied_dve")]
        fz_ready = sem("fz_ready")
        fz_act = sem("fz_act")
        flog_ready = sem("flog_ready")
        fcum_full = sem("fcum_full")
        lam_in = sem("lam_in")
        lam_exp = sem("lam_exp")
        scores_ready = sem("scores_ready")
        shift_ready = sem("shift_ready")
        probs_ready = sem("probs_ready")
        sink_ready = sem("sink_ready")
        mix_ready = sem("mix_ready")
        probsT_ready = sem("probsT_ready")
        probT_copied = [sem("probT_copied_act"), sem("probT_copied_dve")]
        out_ready = sem("out_ready")
        out_copied = sem("out_copied")
        job_out = sem("job_out")
        oT_full = sem("oT_full")
        hid_copied = sem("hid_copied")
        vec_loaded = sem("vec_loaded")
        kc_loaded = sem("kc_loaded")
        vc_loaded = sem("vc_loaded")
        fc_loaded = sem("fc_loaded")
        ple_loaded = sem("ple_loaded")
        pleT_full = sem("pleT_full")
        pleT_copied = sem("pleT_copied")
        stored = sem("stored")
        proj_free = sem("proj_free")
        table_loaded = sem("table_loaded")
        x_loaded = sem("x_loaded")
        x_full = sem("x_full")
        x_copied = sem("x_copied")
        y_full = sem("y_full")
        y_copied = sem("y_copied")
        pad_cleared = sem("pad_cleared")
        cleared = sem("cleared")
        pe_passed = sem("pe_passed")
        pool_passed = sem("pool_passed")
        step = sem("dve_step")

        block = ctx.enter_context(nc.Block())

        UNITS, TAIL0 = 400, 76
        TAIL = UNITS - TAIL0
        SLOT = UNITS // RING
        CHUNKS = 44
        N_RMS = 2 + FG
        SLOPE_A = [2.0 ** -(h + 1) for h in range(8)]
        SLOPE_B = [2.0 ** -(2 * (h + 1)) for h in range(4)]
        WIN = {"A": [(0, 8, 2, 512, 0), (8, 4, 4, 256, 512)],
               "B": [(12, 8, 2, 512, 0), (20, 8, 2, 512, 512), (28, 8, 2, 512, 1024)],
               "C": [(36, 8, 2, 512, 0), (44, 2, 16, 40, 512)],
               "D": [(52, 8, 2, 512, 0), (60, 8, 2, 512, 512), (68, 8, 2, 512, 1024)]}
        WIN_NO = {"A": 0, "B": 2, "C": 5, "D": 7}
        N_WIN = 10
        LAT0 = 46
        NORM = {n: i for i, n in enumerate(["A", "B", "O2", "O3", "C", "L4", "L5", "D"])}
        N_NORM = len(NORM)
        PREP = {}
        for j, g in enumerate(GROUPS):
            PREP[j] = [("q", m) for m in range(MAPS)]
            PREP[j] += [(k, m) for m in (range(1) if g == "A" else range(MAPS)) for k in ("kc", "kn")]
            if j == 4:
                PREP["lat"] = [("cq", 0), ("cq", 1), ("cq", 2), ("ckvc", 0), ("ckvn", 0)]
        ORDER = [0, 1, 2, 3, "lat", 4, 5, 6, 7]
        PREP_BASE, _t = {}, [0, 0]
        for j in ORDER:
            PREP_BASE[j] = tuple(_t)
            n = len(PREP[j])
            _t = [_t[0] + (n + 1) // 2, _t[1] + n // 2]
        PREP_TOT = tuple(_t)
        N_PREP = sum(_t)
        KEXTENT = {"A": HD, "B": HD, "C": CEXT, "D": DEXT}

        def prep_no(j, i):
            return sum(PREP_BASE[j]) + i

        def prep_waits(l, j, n):
            return (l * PREP_TOT[0] + PREP_BASE[j][0] + (n + 1) // 2, l * PREP_TOT[1] + PREP_BASE[j][1] + n // 2)

        def scores(q):
            return psf[:, (q % 2) * 1024:(q % 2) * 1024 + 960]

        def cached_keys(g):
            return WINDOW if g == "A" else PAST

        def samples(g):
            return cached_keys(g) + DSEQ

        def kdT(j):
            return kT[0:KEXTENT[GROUPS[j]], :, :]

        def kext_of(g):
            w = KEXTENT[g]
            return kext[:, :, :, :].rearrange("p a b c -> p (a b c)")[:, 0:7 * MAPS * w].rearrange(
                "p (t m c) -> p t m c", t=7, m=MAPS)

        def qext_of(g):
            w = KEXTENT[g]
            return qext[:, :, :, :].rearrange("p a b c -> p (a b c)")[:, 0:3 * MAPS * w].rearrange(
                "p (t m c) -> p t m c", t=3, m=MAPS)

        def query_src(j, m, t):
            g, hh = GROUPS[j], j % 2
            if g in "AB":
                return proj[:, t, hh * 256 + m * HD:hh * 256 + (m + 1) * HD]
            return qext_of(g)[:, t, m, :]

        def new_key_src(j, m, t):
            g, hh = GROUPS[j], j % 2
            if g == "A":
                return proj[:, t, 512 + hh * HD:512 + (hh + 1) * HD]
            if g == "B":
                return proj[:, t, 512 + hh * 256 + m * HD:512 + hh * 256 + (m + 1) * HD]
            return kext_of(g)[:, (5, 6, 4)[t], m, :]

        def cached_key_src(j, m, t):
            g = GROUPS[j]
            return kcache[:, t, m * HD:(m + 1) * HD] if g in "AB" else kext_of(g)[:, t, m, :]

        def values(j, col, w, t):
            g, hh = GROUPS[j], j % 2
            if g == "C":
                return vtok[:, t, col:col + w]
            if t < 4:
                return vtok[:, t, 0:HD] if g == "A" else vtok[:, t, col:col + w]
            tile = {4: 2, 5: 0, 6: 1}[t]
            if g == "A":
                return proj[:, tile, 640 + hh * HD:640 + (hh + 1) * HD]
            return proj[:, tile, 1024 + hh * 256 + col:1024 + hh * 256 + col + w]

        @block.sync
        def _(sp):
            def load(l, q4, u, dst_cols, src, tail=False):
                s = u % RING
                if tail:
                    sp.wait_ge(lo_ready, l * TAIL + 4 * q4 + u + 1 - TAIL0 - RING)
                else:
                    sp.wait_ge(unit_used, l * UNITS + 4 * q4 + u + 1)
                dst = ring[:, s, 0:dst_cols]
                if len(src.shape) == 3:
                    dst = dst.rearrange("p (a n) -> p a n", a=src.shape[1])
                sp.dma_start(dst, src).then_inc(raw_loaded[s], 16)

            def chunk(l, q4, w, rows, cols, ncol, kb, tail=False):
                for u in range(KB // kb):
                    src = w[l, bass.ds(rows + u * kb * 128, kb * 128), bass.ds(cols, ncol)]
                    load(l, q4, u, kb * ncol, src.rearrange("(a p) n -> p a n", p=128),
                         tail and u >= RING if tail == "first" else tail)

            for tile in range(2):
                sp.dma_start(hid[:, :, :].rearrange("p a b -> p (a b)")[:, tile * DM:(tile + 1) * DM],
                             I["x_prompt"][0, tile * 128:(tile + 1) * 128, :]).then_inc(x_loaded, 16)
            sp.dma_start(arena[0:DSEQ, 0:DM], I["x_sample"][0, :, :]).then_inc(x_loaded, 16)
            with sp.Fori(0, DEPTH) as l:
                w_in = I["w_in"]
                chunk(l, 0, w_in, 0, W_A, 512, 2)
                chunk(l, 2, w_in, 0, W_A + 512, 256, 4)
                for c in range(3):
                    chunk(l, 3 + 2 * c, w_in, 0, W_B + 512 * c, 512, 2)
                chunk(l, 9, w_in, 0, W_CL, 512, 2)
                load(l, 11, 0, 16 * 32, w_in[l, :, W_CR:W_D].rearrange("(a p) n -> p a n", p=128))
                load(l, 11, 1, 16 * 8, w_in[l, :, W_F:W_F + 8].rearrange("(a p) n -> p a n", p=128))
                for hh in range(2):
                    for half in range(2):
                        c0 = hh * 384 + half * 192
                        load(l, 11, 2 + 3 * hh + half, 576,
                             I["c_wq_up"][l, :, c0:c0 + 192].rearrange("(a p) n -> p a n", p=128))
                    load(l, 11, 4 + 3 * hh, 512, I["c_wkv_up"][l, :, hh * 512:(hh + 1) * 512])
                for c in range(3):
                    chunk(l, 13 + 2 * c, w_in, 0, W_D + 512 * c, 512, 2)
                chunk(l, 19, I["w_out"], 0, 0, 512, 2, "first")
                with sp.Fori(1, 4) as c:
                    chunk(l, 19 + 2 * c, I["w_out"], 0, 512 * c, 512, 2, True)
                with sp.Fori(0, FG) as g:
                    with sp.Fori(0, 4) as c:
                        chunk(l, 27 + 16 * g + 2 * c, I["w_up"], 0, DM * g + 512 * c, 512, 2, True)
                    with sp.Fori(0, 4) as c:
                        chunk(l, 35 + 16 * g + 2 * c, I["w_down"], DM * g, 512 * c, 512, 2, True)
                for c in range(4):
                    load(l, 91, c, 1024, I["w_ple"][l, :, 512 * c:512 * (c + 1)].rearrange("(a p) n -> p a n", p=128),
                         True)
                with sp.Fori(0, 4) as c:
                    chunk(l, 92 + 2 * c, I["w_ple_gate"], 0, 512 * c, 512, 2, True)
            for tile in range(2):
                sp.wait_ge(y_copied, 4 * (tile + 1))
                sp.dma_start(O["y_prompt"][0, tile * 128:(tile + 1) * 128, :],
                             hid[:, :, :].rearrange("p a b -> p (a b)")[:, tile * DM:(tile + 1) * DM]).then_inc(x_loaded, 16)
            sp.wait_ge(y_copied, 12)
            sp.dma_start(O["y_sample"][0, :, :], arena[0:DSEQ, 0:DM]).then_inc(x_loaded, 16)
            sp.wait_ge(x_loaded, 96)

        STORED = (6, 10, 14, 20)
        N_STORED = STORED[-1]

        @block.gpsimd
        def _(pool):
            def hold(s, value):
                pool.wait_ge(s, value)
                pool.sem_inc(pool_passed, 1)

            pool.dma_start(table[:, :], I["table"]).then_inc(table_loaded, 16)
            pool.sem_inc(proj_free, 1)
            for t, val in ((ones[:, :], 1.0), (eps[:, :], EPS), (xg[:, KB * TOK:], 0.0),
                           (acc[:, TOK:], 0.0), (mx[:, :, :], 0.0), (flog[:, :, :], 0.0)):
                nc.gpsimd.memset(t, val)
            nc.gpsimd.memset(sums[:, :, :], 1.0).then_inc(cleared, 1)
            with pool.Fori(0, DEPTH) as l:
                hold(job_out, l * 8 + 1)
                hold(half_free, l * CHUNKS + 2)
                nc.gpsimd.memset(cqT_pad, 0.0).then_inc(pad_cleared, 1)
                for name, w in VECS:
                    src = I[name][l, :] if name != "lam_init" else I["lam_init"][l, :]
                    pool.dma_start(vec[:, VOFF[name]:VOFF[name] + w], src.partition_broadcast(128)).then_inc(vec_loaded, 16)
                with nc.allow_non_contiguous_dma("feature-major gains"):
                    for i, name in enumerate(("g_mix", "g_mlp", "g_ple")):
                        pool.dma_start(gains[:, i, :], I[name][l, :].rearrange("(a p) -> p a", p=128)).then_inc(vec_loaded, 16)
                pool.dma_start(flog[:, 0:4, :], I["cache_d_logf"][l, 0, :, :].rearrange("(t p) h -> p t h", p=128))\
                    .then_inc(fc_loaded, 16)

                def loads(j):
                    g, hh = GROUPS[j], j % 2
                    if j:
                        hold(prep_full, l * N_PREP + prep_no(j - 1, len(PREP[j - 1])))
                    if g == "A":
                        pool.dma_start(kcache[:, 3, 0:HD], I["cache_a_k"][l, 0, :, hh, :]).then_inc(kc_loaded, 16)
                    elif g in "BD":
                        src = (I["cache_b_k"][l, 0].rearrange("(t p) h c d -> p t (h c d)", p=128) if g == "B"
                               else I["cache_d_k"][l, 0].rearrange("(t p) h d -> p t (h d)", p=128))
                        pool.dma_start(kcache[:, :, :], src[:, :, hh * 256:(hh + 1) * 256]).then_inc(kc_loaded, 16)
                    elif hh == 0:
                        pool.dma_start(kcache[:, :, 0:CKVR], I["cache_c_kv"][l, 0].rearrange("(t p) d -> p t d", p=128))\
                            .then_inc(kc_loaded, 16)
                        pool.dma_start(kcache[:, :, CKVR:CKVR + ROPE],
                                       I["cache_c_krope"][l, 0].rearrange("(t p) d -> p t d", p=128)).then_inc(kc_loaded, 16)
                    hold(job_out, l * 8 + j + 1)
                    if g == "A":
                        pool.dma_start(vtok[:, 3, 0:HD], I["cache_a_v"][l, 0, :, hh, :]).then_inc(vc_loaded, 16)
                    elif g in "BD":
                        src = (I["cache_b_v"][l, 0].rearrange("(t p) h d -> p t (h d)", p=128) if g == "B"
                               else I["cache_d_v"][l, 0].rearrange("(t p) h d -> p t (h d)", p=128))
                        pool.dma_start(vtok[:, 0:4, :], src[:, :, hh * 256:(hh + 1) * 256]).then_inc(vc_loaded, 16)

                def store(dst, src):
                    pool.dma_start(dst, src).then_inc(stored, 16)

                def store_group(n, pairs):
                    hold(group_ready, l * 4 + n + 1)
                    for out_p, out_s, c, w in pairs:
                        store(out_p.rearrange("(t p) n -> p t n", p=128), proj[:, 0:2, c:c + w])
                        store(out_s, proj[0:DSEQ, 2, c:c + w])

                def stored_group(n):
                    pool.wait_ge(stored, 16 * (l * N_STORED + STORED[n]))
                    pool.sem_inc(proj_free, 1)

                loads(0)
                hold(group_ready, l * 4 + 1)
                for out_p, out_s, cache, c in (("a_k_p", "a_k_s", "cache_a_k", 512), ("a_v_p", "a_v_s", "cache_a_v", 640)):
                    store(O[out_p][l, 0].rearrange("t h d -> t (h d)"), proj[:, 1, c:c + 128])
                    store(O[out_s][l, 0, DSEQ:WINDOW].rearrange("t h d -> t (h d)"), proj[0:DSEQ, 2, c:c + 128])
                    store(O[out_s][l, 0, 0:DSEQ].rearrange("t h d -> t (h d)"),
                          I[cache][l, 0, DSEQ:WINDOW].rearrange("t h d -> t (h d)"))
                loads(1)
                stored_group(0)
                loads(2)
                store_group(1, [(O["b_k_p"][l, 0].rearrange("t h c d -> t (h c d)"),
                                 O["b_k_s"][l, 0].rearrange("t h c d -> t (h c d)"), 512, 512),
                                (O["b_v_p"][l, 0].rearrange("t h d -> t (h d)"),
                                 O["b_v_s"][l, 0].rearrange("t h d -> t (h d)"), 1024, 512)])
                loads(3)
                stored_group(1)
                loads(4)
                store_group(2, [(O["c_kv_p"][l, 0], O["c_kv_s"][l, 0], CQR, CKVR),
                                (O["c_krope_p"][l, 0], O["c_krope_s"][l, 0], 512, ROPE)])
                loads(5)
                stored_group(2)
                loads(6)
                store_group(3, [(O["d_k_p"][l, 0].rearrange("t h d -> t (h d)"),
                                 O["d_k_s"][l, 0].rearrange("t h d -> t (h d)"), 512, 512),
                                (O["d_v_p"][l, 0].rearrange("t h d -> t (h d)"),
                                 O["d_v_s"][l, 0].rearrange("t h d -> t (h d)"), 1024, 512)])
                store(O["d_logf_p"][l, 0].rearrange("(t p) h -> p t h", p=128), flog[:, 5:7, :])
                store(O["d_logf_s"][l, 0], flog[0:DSEQ, 4, :])
                loads(7)
                stored_group(3)
                hold(job_out, l * 8 + 9)
                pool.dma_start(otmp[:, 0:2, :], I["p_prompt"][l, 0].rearrange("(t p) n -> p t n", p=128)).then_inc(ple_loaded, 16)
                pool.dma_start(otmp[0:DSEQ, 2, :], I["p_sample"][l, 0]).then_inc(ple_loaded, 16)
                with pool.Fori(0, TAIL // RING) as u4:
                    for s in range(RING):
                        hold(hi_ready, l * TAIL + RING * u4 + s + 1)
                        nc.gpsimd.tensor_tensor(wlo[:, s, :], ring[:, s, :], whi[:, s, :].bitcast(f32), ALU.subtract)\
                            .then_inc(lo_ready, 1)
            hold(stored, 16 * N_STORED * DEPTH)

        N_VEC = len(VECS) + 3
        KC = [1, 2, 3, 4, 6, 6, 7, 8]
        VC = [1, 2, 3, 4, 4, 4, 5, 6]

        @block.tensor
        def _(pe):
            mm = nc.tensor.matmul

            def hold(s, value):
                pe.wait_ge(s, value)
                pe.sem_inc(pe_passed, 1)

            def unit(l, q4, u):
                hold(raw_loaded[u % RING], 16 * (l * SLOT + q4 + u // RING + 1))
                return ring[:, u % RING, :]

            def tail_unit(l, q4, u):
                hold(lo_ready, l * TAIL + 4 * q4 + u + 1 - TAIL0)
                return [w[:, u % RING, :].rearrange("p (a n) -> p a n", a=UK) for w in (whi, wlo)]

            def product(out, w, k, m, x2, start, stop):
                (hi, lo), (xh, xl), cols = w, x2, slice(m * 128, (m + 1) * 128)
                mm(out, lo[:, k, cols], xh, start=start, stop=False)
                mm(out, hi[:, k, cols], xl, start=False, stop=False)
                return mm(out, hi[:, k, cols], xh, start=False, stop=stop)

            def gemm_chunk(l, q4, half, chunk_no, src, before_unit=None, before_last=None):
                units, nk = KB // UK, UK
                hold(half_free, l * CHUNKS + chunk_no + 1)
                for u in range(units):
                    w = tail_unit(l, q4, u)
                    if before_unit:
                        before_unit(u)
                    for m in range(4):
                        if m == 3 and u == 0 and before_last:
                            before_last()
                        for k in range(nk):
                            last = product(ps[:, 4 * half + m, 0:TOK], w, k, m, src(u * nk + k),
                                           u == 0 and k == 0, u == units - 1 and k == nk - 1)
                        if u == units - 1 and m < 3:
                            last.then_inc(bank_full, 1)
                    last.then_inc(unit_used, 1)

            def x_block(k):
                return xhi[:, k, :], xlo[:, k, :]

            def hid_block(k):
                return hhi[:, k, :], hlo[:, k, :]

            def rms_feature(l, p, half):
                hold(acc_ready, l * 3 + p + 1)
                mm(ps[:, 4 * half + 3, 0:TOK], ones[:, :], acc[:, 0:TOK], start=True, stop=True).then_inc(rms_summed, 1)

            def w_in_chunk(l, c, no, first=False):
                n0, units, nk, ncol, _ = c
                half = no % 2
                for u in range(units):
                    w = unit(l, n0 // 4, (n0 % 4) + u)
                    if first:
                        hold(gained, l * KB + min(KB, (u + 1) * nk + 1))
                    for t in range(3):
                        if ncol == 40:
                            n = (32, 8)[u]
                            wv = w[:, 0:16 * n].rearrange("p (a n) -> p a n", a=16)
                            for k in range(nk):
                                last = mm(ps[:, 4 * half + t, 32 * u:32 * u + n], xg[:, k * TOK + t * 128:k * TOK + t * 128 + 128],
                                          wv[:, k, :], start=(k == 0), stop=(k == nk - 1))
                        else:
                            wv = w[:, 0:nk * ncol].rearrange("p (a n) -> p a n", a=nk)
                            for k in range(nk):
                                kk = u * nk + k
                                last = mm(ps[:, 4 * half + t, 0:ncol], xg[:, kk * TOK + t * 128:kk * TOK + t * 128 + 128],
                                          wv[:, k, :], start=(kk == 0), stop=(kk == KB - 1))
                        if u == units - 1 and t < 2:
                            last.then_inc(proj_full, 1)
                    last.then_inc(unit_used, 1)

            def tr(out, in_):
                return nc.tensor.transpose(out, in_, ident[0:in_.shape[0], 0:in_.shape[0]])

            def prep(l, j):
                g = GROUPS[j] if j != "lat" else None
                for i, (what, m) in enumerate(PREP[j]):
                    b = i % 8
                    if i >= 8:
                        a, d = prep_waits(l, j, i - 7)
                        hold(prep_copied[i % 2], (a, d)[i % 2])
                    if what in ("q", "cq", "kn", "ckvn"):
                        src = {"q": lambda t: query_src(j, m, t), "kn": lambda t: new_key_src(j, m, t),
                               "cq": lambda t: proj[:, t, m * 128:(m + 1) * 128],
                               "ckvn": lambda t: proj[:, t, CQR:CQR + CKVR]}[what]
                        w = src(0).shape[1]
                        o = DSEQ if what in ("kn", "ckvn") else 0
                        tr(ps[0:w, b, o:o + 128], src(0)[:, :])
                        tr(ps[0:w, b, o + 128:o + 256], src(1)[:, :])
                        s = 0 if o else 256
                        tr(ps[0:w, b, s:s + DSEQ], src(2)[0:DSEQ, :]).then_inc(prep_full, 1)
                    else:
                        for t in range(3 if g == "A" else 0, 4):
                            src = kcache[:, t, 0:CKVR] if what == "ckvc" else cached_key_src(j, m, t)
                            last = tr(ps[0:src.shape[1], b, t * 128:(t + 1) * 128], src)
                        last.then_inc(prep_full, 1)

            def latents(l, j):
                hh = j - 4
                hold(pad_cleared, l + 1)
                a, d = prep_waits(l, "lat", len(PREP["lat"]))
                hold(prep_copied[0], a)
                hold(prep_copied[1], d)
                if hh:
                    hold(hid_copied, l * 16 + 2 * j)
                w = [unit(l, 11, 2 + 3 * hh + i)[:, 0:576].rearrange("p (a n) -> p a n", a=3) for i in range(2)]
                for t in range(3):
                    for i in range(2):
                        for k in range(3):
                            last = mm(ps[:, t, i * 192:(i + 1) * 192], cqT[:, k * TOK + t * 128:k * TOK + t * 128 + 128],
                                      w[i][:, k, :], start=(k == 0), stop=(k == 2))
                    if t < 2:
                        last.then_inc(lat_full, 1)
                    else:
                        last.then_inc(unit_used, 2)
                hold(raw_loaded[(4 + 3 * hh) % RING], 16 * (l * SLOT + 11 + (4 + 3 * hh) // RING + 1))
                wk = ring[:, (4 + 3 * hh) % RING, 0:512]
                for i in range(7):
                    off = i * 128 if i < 5 else KEYS + (i - 5) * 128
                    b = 3 + i if i < 5 else i - 5
                    if i >= 5:
                        hold(lat_copied[1], l * 12 + 6 * hh + i - 4)
                    last = mm(ps[:, b, :], ckvT[:, off:off + 128], wk, start=True, stop=True)
                    if i < 6:
                        last.then_inc(lat_full, 1)
                last.then_inc(unit_used, 1)

            def score_map(l, q):
                j, m = q // MAPS, q % MAPS
                g = GROUPS[j]
                S, K, km = scores(q), KEXTENT[g], (0 if g == "A" else m)
                k0, ns = PAST - cached_keys(g), samples(g)
                if m >= 2:
                    hold(probs_ready, l * N_MAPS + q - 1)
                kk = kT[0:K, km, :]
                n0 = min(ns, 512)
                qs = qT[0:K, m, 256:TOK]
                mm(S[0:DSEQ, 0:n0], qs, kk[:, k0:k0 + n0], start=True, stop=True)
                if ns > 512:
                    mm(S[0:DSEQ, 512:ns], qs, kk[:, k0 + 512:k0 + ns], start=True, stop=True)
                mm(S[:, 576:704], qT[0:K, m, 0:128], kk[:, KEYS:KEYS + 128], start=True, stop=True)
                mm(S[:, 704:960], qT[0:K, m, 128:256], kk[:, KEYS:KEYS + 256], start=True, stop=True)\
                    .then_inc(scores_ready, 1)

            def transpose_probs(l, it):
                j, maps, _, _ = ITEMS[it]
                g = GROUPS[j]
                q = j * MAPS + maps[0]
                if g == "B":
                    hold(mix_ready, l * 4 + (it - 8) + 1)
                else:
                    hold(probs_ready, l * N_MAPS + q + 1)
                if it:
                    hold(probT_copied[0], l * N_ITEMS + it)
                    hold(probT_copied[1], l * N_ITEMS + it)
                P = prob[:, q % 4, :]
                tr(ps[:, 4, 0:128], P[:, 576:704])
                tr(ps[:, 4, 128:256], P[:, 704:832])
                tr(ps[:, 4, 256:384], P[:, 832:960])
                nb = cached_keys(g) // 128
                for i in range(nb):
                    tr(ps[:, 5, i * 64:(i + 1) * 64], P[0:DSEQ, i * 128:(i + 1) * 128])
                tr(ps[0:DSEQ, 5, nb * 64:(nb + 1) * 64], P[0:DSEQ, nb * 128:nb * 128 + 64]).then_inc(probsT_ready, 1)

            def weigh_values(l, it):
                j, maps, col, w = ITEMS[it]
                g = GROUPS[j]
                hold(probT_copied[0], l * N_ITEMS + it + 1)
                hold(probT_copied[1], l * N_ITEMS + it + 1)
                if it:
                    hold(out_copied, l * N_ITEMS + it)
                nb = cached_keys(g) // 128
                for i in range(nb):
                    mm(ps[0:DSEQ, 6, 0:w], probT[:, 384 + i * 64:384 + (i + 1) * 64], values(j, col, w, 4 - nb + i),
                       start=(i == 0), stop=False)
                mm(ps[0:DSEQ, 6, 0:w], probT[0:DSEQ, 384 + nb * 64:384 + (nb + 1) * 64],
                   values(j, col, w, 4)[0:DSEQ, :], start=False, stop=True)
                mm(ps[:, 6, w:2 * w], probT[:, 0:128], values(j, col, w, 5), start=True, stop=True)
                mm(ps[:, 6, 2 * w:3 * w], probT[:, 128:256], values(j, col, w, 5), start=True, stop=False)
                mm(ps[:, 6, 2 * w:3 * w], probT[:, 256:384], values(j, col, w, 6), start=False, stop=True)\
                    .then_inc(out_ready, 1)

            def attention(l, j):
                g = GROUPS[j]
                hold(vc_loaded, 16 * (l * VC[-1] + VC[j]))
                its = [i for i, it in enumerate(ITEMS) if it[0] == j]
                a, d = prep_waits(l, j, len(PREP[j]))
                hold(prep_copied[0], a)
                hold(prep_copied[1], d)
                for m in ITEMS[its[0]][1]:
                    score_map(l, j * MAPS + m)
                for it in its:
                    if it + 1 in its:
                        for m in ITEMS[it + 1][1]:
                            score_map(l, j * MAPS + m)
                    transpose_probs(l, it)
                    weigh_values(l, it)
                hold(job_out, l * 8 + j + 2)
                for fb in range(2):
                    b = 7 - fb
                    for t, o, n in ((0, 256, DSEQ), (1, 0, 128), (2, 128, 128)):
                        last = tr(ps[:, b, o:o + n], otok[0:n, t, fb * 128:(fb + 1) * 128])
                    last.then_inc(oT_full, 1)

            hold(table_loaded, 16)
            hold(cleared, 1)
            hold(x_loaded, 48)
            hold(x_copied, 1)
            hflat = hid[:, :, :].rearrange("p a b -> p (a b)")
            for k in range(KB):
                if k >= 8:
                    hold(x_copied, k - 8 + 2)
                tr(ps[:, k % 8, 0:128], hflat[:, k * 128:(k + 1) * 128])
                tr(ps[:, k % 8, 128:256], hflat[:, DM + k * 128:DM + (k + 1) * 128])
                tr(ps[:, k % 8, 256:TOK], arena[0:DSEQ, k * 128:(k + 1) * 128]).then_inc(x_full, 1)
            pe.sem_inc(unit_used, RING)
            with pe.Fori(0, DEPTH) as l:
                hold(half_free, l * CHUNKS + 2)
                for g in "ABCD":
                    if g != "A":
                        hold(hid_copied, l * 16 + {"B": 4, "C": 8, "D": 12}[g])
                    for i, c in enumerate(WIN[g]):
                        no = WIN_NO[g] + i
                        if i >= 2:
                            hold(proj_copied, l * N_WIN + no - 1)
                        w_in_chunk(l, c, no, first=(no == 0))
                        if no == 0:
                            hold(acc_ready, l * 3 + 1)
                            for t in range(3):
                                last = mm(ps[:, 3, t:t + 1], acc[:, t * 128:(t + 1) * 128], ones[:, 0:1], start=True, stop=True)
                            last.then_inc(rms_summed, 1)
                    if g == "C":
                        hold(proj_copied, l * N_WIN + 7)
                        hold(group_ready, l * 4 + 3)
                        hold(kc_loaded, 16 * (l * KC[-1] + KC[4]))
                        prep(l, "lat")
                    if g == "D":
                        hold(flog_ready, l + 1)
                        hold(fc_loaded, 16 * (l + 1))
                        hold(proj_copied, l * N_WIN + 10)
                        for tiles in ([0, 1, 2, 3, 4], [5, 6]):
                            for n, t in enumerate(tiles):
                                rows = DSEQ if t == 4 else 128
                                for e in tiles[:n]:
                                    mm(ps[:, 0, t * 8:(t + 1) * 8], ones[:, :], flog[:, e, :], start=(e == tiles[0]), stop=False)
                                last = mm(ps[:, 0, t * 8:(t + 1) * 8], tri[0:rows, :], flog[0:rows, t, :], start=(n == 0), stop=True)
                        last.then_inc(fcum_full, 1)
                    for j in [jj for jj, gg in enumerate(GROUPS) if gg == g]:
                        if g == "C":
                            latents(l, j)
                        if j % 2 or g in "CD":
                            if g != "C":
                                hold(hid_copied, l * 16 + 2 * j)
                        if g in "AB":
                            hold(kc_loaded, 16 * (l * KC[-1] + KC[j]))
                            hold(group_ready, l * 4 + "ABCD".index(g) + 1)
                        else:
                            hold(ext_ready, l * 4 + j - 3)
                        prep(l, j)
                        attention(l, j)
                hold(hid_copied, (l + 1) * 16)
                with pe.Fori(0, 2) as c2:
                    for h in range(2):
                        gemm_chunk(l, 19 + 4 * c2 + 2 * h, h, c2 * 2 + h, hid_block,
                                   before_unit=lambda u: hold(split_ready, l * 48 + 2 * u + 2))
                with pe.Fori(0, FG) as g:
                    for c in range(4):
                        gemm_chunk(l, 27 + 16 * g + 2 * c, c % 2, 4 + 8 * g + c, x_block,
                                   before_unit=(lambda u: hold(split_ready, l * 48 + 16 + 2 * u + 2)) if c == 0 else None,
                                   before_last=(lambda: hold(rms_ready, l * N_RMS + g + 2)) if c == 1 else None)
                        if c == 0:
                            hold(half_free, l * CHUNKS + 8 * g + 6)
                            rms_feature(l, 1, 1)
                    for c in range(4):
                        gemm_chunk(l, 35 + 16 * g + 2 * c, c % 2, 8 + 8 * g + c, hid_block,
                                   before_unit=(lambda u: hold(hid_ready, l * 64 + g * 16 + 2 * u + 2)) if c == 0 else None)
                hold(ple_loaded, 32 * (l + 1))
                hold(half_free, l * CHUNKS + 38)
                for fb in range(2):
                    for t, o, n in ((0, 0, 128), (1, 128, 128), (2, 256, DSEQ)):
                        last = tr(ps[:, 4 + fb, o:o + n], otmp[0:n, t, fb * 128:(fb + 1) * 128])
                last.then_inc(pleT_full, 1)
                hold(pleT_copied, l + 1)
                for c in range(4):
                    hold(half_free, l * CHUNKS + 36 + c + 1)
                    w = tail_unit(l, 91, c)
                    for m in range(4):
                        for k in range(2):
                            last = product(ps[:, 4 * (c % 2) + m, 0:TOK], w, k, m, (pleh[:, k, :], plel[:, k, :]),
                                           k == 0, k == 1)
                        last.then_inc(bank_full if m < 3 else unit_used, 1)
                for c in range(4):
                    gemm_chunk(l, 92 + 2 * c, c % 2, 40 + c, x_block,
                               before_unit=(lambda u: hold(split_ready, l * 48 + 32 + 2 * u + 2)) if c == 0 else None,
                               before_last=(lambda: hold(rms_ready, l * N_RMS + N_RMS)) if c == 1 else None)
                    if c == 0:
                        hold(half_free, l * CHUNKS + 42)
                        rms_feature(l, 2, 1)
            hold(half_free, DEPTH * CHUNKS + 2)
            for i in range(12):
                t, q = i // 4, i % 4
                if i >= 8:
                    hold(y_copied, i - 7)
                n = 128 if t < 2 else DSEQ
                for k in range(4):
                    last = tr(ps[0:n, i % 8, k * 128:(k + 1) * 128], x[:, q * 4 + k, t * 128:t * 128 + n])
                last.then_inc(y_full, 1)

        def norm_views(name):
            if name in "ABD":
                h = 10 if name == "A" else 16
                return [(proj[:, :, 0:h * HD].rearrange("p t (h d) -> p t h d", d=HD), 3, h, HD, 0)]
            if name == "C":
                return [(proj[:, :, a:a + w].rearrange("p t (h d) -> p t h d", d=w), 3, 1, w, 3 * i)
                        for i, (a, w) in enumerate(((0, CQR), (CQR, CKVR), (512, ROPE)))]
            if name[0] == "L":
                return [(kext[:, :, :, 0:HD], 7, MAPS, HD, 0), (qext[:, :, :, 0:HD], 3, MAPS, HD, 28),
                        (qext[:, :, :, HD:CEXT], 3, MAPS, ROPE, 40)]
            return [(otok[:, :, :].rearrange("p t (h d) -> p t h d", d=128), 3, 2, 128, 0)]

        def sq_views(name):
            out, at = [], 0
            for _, t, h, w, _ in norm_views(name):
                out.append(sq[:, at:at + t * h * w].rearrange("p (t h d) -> p t h d", t=t, h=h))
                at += t * h * w
            return out

        def prep_target(j, what, m, b):
            if what == "cq":
                return cqT[:, m * TOK:(m + 1) * TOK], ps[:, b, 0:TOK]
            if what == "ckvc":
                return ckvT[:, 0:PAST], ps[:, b, 0:PAST]
            if what == "ckvn":
                return ckvT[:, PAST:ALLK], ps[:, b, 0:TOK]
            K = KEXTENT[GROUPS[j]]
            if what == "q":
                return qT[0:K, m, :], ps[0:K, b, 0:TOK]
            if what == "kn":
                return kT[0:K, m, PAST:ALLK], ps[0:K, b, 0:TOK]
            k0 = PAST - cached_keys(GROUPS[j])
            return kT[0:K, m, k0:PAST], ps[0:K, b, k0:PAST]

        def scale_of(g):
            return CEXT ** -0.5 if g == "C" else HD ** -0.5

        @block.scalar
        def _(act):
            A = nc.scalar.activation

            def gain_pass(l):
                act.wait_ge(half_free, l * CHUNKS + 2)
                for b in range(KB):
                    A(xg[:, b * TOK:(b + 1) * TOK], x[:, b, :], ACT.Copy, scale=gains[:, 0, b:b + 1]).then_inc(gained, 1)

            def upper_halves(l, n):
                for s in range(RING):
                    act.wait_ge(raw_loaded[s], 16 * (l * SLOT + n + 1))
                    act.wait_ge(unit_used, l * UNITS + RING * n + s + 1)
                    A(whi[:, s, :], ring[:, s, :], ACT.Copy).then_inc(hi_ready, 1)

            def sigmoids(l, c):
                for b in range(4 * c, 4 * c + 4):
                    act.wait_ge(sig_in, l * 16 + b + 1)
                    A(t1[:, b % 2, :], t0[:, b % 2, :], ACT.Sigmoid).then_inc(sig_ready, 1)

            def rms_root(l, n, src, dst):
                act.wait_ge(rms_summed, l * N_RMS + n + 1)
                A(dst, src, ACT.Sqrt, bias=eps[:, 0:1], scale=1.0 / DM).then_inc(rms_ready, 1)

            def norm(l, name):
                n = l * N_NORM + NORM[name] + 1
                for (src, t, h, w, _), dst in zip(norm_views(name), sq_views(name)):
                    last = A(dst, src, ACT.Square)
                last.then_inc(sq_ready, 1)
                act.wait_ge(ssq_ready, n)
                spans = {}
                for _, t, h, w, o in norm_views(name):
                    lo, hi = spans.get(w, (o, o))
                    spans[w] = (min(lo, o), max(hi, o + t * h))
                for w, (lo, hi) in spans.items():
                    last = A(root[:, lo:hi], ssq[:, lo:hi], ACT.Sqrt, bias=eps[:, 0:1], scale=1.0 / w)
                last.then_inc(root_ready, 1)

            def prep(l, j):
                for i in range(0, len(PREP[j]), 2):
                    what, m = PREP[j][i]
                    act.wait_ge(prep_full, l * N_PREP + prep_no(j, i) + 1)
                    dst, src = prep_target(j, what, m, i % 8)
                    A(dst, src, ACT.Copy).then_inc(prep_copied[0], 1)

            def exps(l, it):
                j, maps, _, _ = ITEMS[it]
                g = GROUPS[j]
                for m in maps:
                    q = j * MAPS + m
                    S, P, ns = scores(q), prob[:, q % 4, :], samples(g)
                    act.wait_ge(shift_ready, l * N_MAPS + q + 1)
                    if it >= 2:
                        act.wait_ge(probsT_ready, l * N_ITEMS + it - 1)
                    if g == "A":
                        act.wait_ge(sink_ready, l * 8 + q + 1)
                        A(es[:, q, :], es[:, q, :], ACT.Exp, scale=scale_of(g))
                    for t, (lo, hi, n) in enumerate(((0, ns, DSEQ), (576, 704, 128), (704, 960, 128))):
                        last = A(P[0:n, lo:hi], S[0:n, lo:hi], ACT.Exp, bias=sm[0:n, q, t:t + 1], scale=scale_of(g),
                                 accum_out=sums[0:n, q, t:t + 1])
                    last.then_inc(probs_ready, 1)

            def attention(l, j):
                its = [i for i, it in enumerate(ITEMS) if it[0] == j]
                exps(l, its[0])
                nb = cached_keys(GROUPS[j]) // 128
                for it in its:
                    if it + 1 in its:
                        exps(l, it + 1)
                    act.wait_ge(probsT_ready, l * N_ITEMS + it + 1)
                    if it:
                        act.wait_ge(out_ready, l * N_ITEMS + it)
                    A(probT[:, 384:384 + nb * 64], ps[:, 5, 0:nb * 64], ACT.Copy)
                    A(probT[0:DSEQ, 384 + nb * 64:448 + nb * 64], ps[0:DSEQ, 5, nb * 64:nb * 64 + 64], ACT.Copy)\
                        .then_inc(probT_copied[0], 1)
                if GROUPS[j] == "B":
                    act.wait_ge(out_copied, l * N_ITEMS + its[-1] + 1)
                    norm(l, f"O{j}")
                for fb in range(2):
                    act.wait_ge(oT_full, l * 16 + 2 * j + fb + 1)
                    A(hid[:, 2 * j + fb, :], ps[:, 7 - fb, 0:TOK], ACT.Copy).then_inc(hid_copied, 1)

            act.wait_ge(cleared, 1)
            with act.Fori(0, DEPTH) as l:
                act.wait_ge(vec_loaded, 16 * N_VEC * (l + 1))
                gain_pass(l)
                rms_root(l, 0, ps[:, 3, 0:3], rroot[:, 0:3])
                act.wait_ge(proj_copied, l * N_WIN + 2)
                norm(l, "A")
                for j, g in enumerate(GROUPS):
                    if j == 2:
                        act.wait_ge(lam_in, l + 1)
                        A(lam[:, 2:4], lam[:, 0:2], ACT.Exp).then_inc(lam_exp, 1)
                        act.wait_ge(proj_copied, l * N_WIN + 5)
                        norm(l, "B")
                    if j == 4:
                        act.wait_ge(proj_copied, l * N_WIN + 7)
                        norm(l, "C")
                        act.wait_ge(fz_ready, 2 * l + 1)
                        A(fsm[:, 2, :], fsm[:, 1, :], ACT.Exp, scale=-1.0).then_inc(fz_act, 1)
                        act.wait_ge(fz_ready, 2 * l + 2)
                        A(fsm[:, 5, :], fsm[:, 3, :], ACT.Ln).then_inc(fz_act, 1)
                        prep(l, "lat")
                    if g == "C":
                        hh = j - 4
                        for i in range(0, 7, 2):
                            if i < 6:
                                act.wait_ge(lat_full, l * 16 + 8 * hh + 2 + i + 1)
                            else:
                                act.wait_ge(unit_used, l * UNITS + LAT0 + 3 * hh + 3 + RING)
                            b = 3 + i if i < 5 else i - 5
                            src = ps[:, b, :].rearrange("p (m d) -> p m d", m=MAPS)
                            A(kext[:, i, :, 0:HD], src[:, :, 0:HD], ACT.Copy)
                            A(vtok[:, i, :].rearrange("p (m d) -> p m d", m=MAPS), src[:, :, HD:128], ACT.Copy)\
                                .then_inc(lat_copied[0], 1)
                        act.wait_ge(lat_copied[1], l * 12 + 6 * hh + 6)
                        act.wait_ge(lat_copied[0], l * 8 + 4 * hh + 4)
                        norm(l, f"L{j}")
                    if j == 6:
                        act.wait_ge(proj_copied, l * N_WIN + 10)
                        norm(l, "D")
                    prep(l, j)
                    attention(l, j)
                with act.Fori(0, 8) as i:
                    upper_halves(l, 19 + i)
                with act.Fori(0, FG) as g:
                    with act.Fori(0, 3) as i:
                        upper_halves(l, 27 + 16 * g + i)
                    rms_root(l, 1 + g, ps[:, 7, 0:TOK], rroot[:, :])
                    with act.Fori(3, 16) as i:
                        upper_halves(l, 27 + 16 * g + i)
                for i in range(9):
                    upper_halves(l, 91 + i)
                    if i and i % 2 == 1 and i > 2:
                        c = (i - 3) // 2
                        if c == 0:
                            rms_root(l, 1 + FG, ps[:, 7, 0:TOK], rroot[:, :])
                        sigmoids(l, c)
                sigmoids(l, 3)

        @block.vector
        def _(dve):
            V = nc.vector
            STEPS = 1024
            count = [0]

            def done(ins):
                count[0] += 1
                ins.then_inc(step, 1)
                dve.wait_ge(step, here[0] + count[0])

            here = [None]

            def mul(out, a, b):
                return V.tensor_tensor(out, a, b, ALU.mult)

            def add(out, a, b):
                return V.tensor_tensor(out, a, b, ALU.add)

            def squares_pass(l, chunks):
                dve.wait_ge(half_free, l * CHUNKS + 2 + chunks)
                done(mul(hid[:, :, :], x[:, :, :], x[:, :, :]))
                V.tensor_reduce(acc[:, 0:TOK], hid[:, :, :].rearrange("p b t -> p t b"), X, ALU.add).then_inc(acc_ready, 1)

            def gain_split(l, p, chunks):
                dve.wait_ge(half_free, l * CHUNKS + 2 + chunks)
                for b in range(0, KB, 2):
                    for i in range(2):
                        last = V.tensor_scalar(xhi[:, b + i, :], x[:, b + i, :], gains[:, p, b + i:b + i + 1], None, ALU.mult)
                    done(last)
                    for i in range(2):
                        V.scalar_tensor_tensor(out=xlo[:, b + i, :], in0=x[:, b + i, :], scalar=gains[:, p, b + i:b + i + 1],
                                               in1=xhi[:, b + i, :].bitcast(f32), op0=ALU.mult, op1=ALU.subtract)\
                            .then_inc(split_ready, 1)

            def w_in_chunks(l, g):
                for i, (n0, units, nk, ncol, c0) in enumerate(WIN[g]):
                    no = WIN_NO[g] + i
                    if i == 0:
                        dve.wait_ge(proj_free, l * 4 + "ABCD".index(g) + 1)
                    for t in range(3):
                        if t < 2:
                            dve.wait_ge(proj_full, l * 2 * N_WIN + 2 * no + t + 1)
                        else:
                            dve.wait_ge(unit_used, l * UNITS + n0 + units + RING)
                        if no == 0 and t == 0:
                            dve.wait_ge(rms_ready, l * N_RMS + 1)
                            done(V.reciprocal(rtok[:, :], rroot[:, 0:3]))
                        last = V.tensor_scalar(proj[:, t, c0:c0 + ncol], ps[:, 4 * (no % 2) + t, 0:ncol],
                                               rtok[:, t:t + 1], None, ALU.mult)
                    last.then_inc(proj_copied, 1)

            def norm(l, name):
                n = l * N_NORM + NORM[name] + 1
                dve.wait_ge(sq_ready, n)
                for (_, t, h, w, o), s in zip(norm_views(name), sq_views(name)):
                    last = V.tensor_reduce(ssq[:, o:o + t * h], s, X, ALU.add)
                last.then_inc(ssq_ready, 1)
                tot = sum(t * h for _, t, h, _, _ in norm_views(name))
                dve.wait_ge(root_ready, n)
                done(V.reciprocal(rstd[:, 0:tot], root[:, 0:tot]))
                for view, t, h, w, o in norm_views(name):
                    r = rstd[:, o:o + t * h].rearrange("p (t h) -> p t h", t=t).unsqueeze(3).broadcast_to([128, t, h, w])
                    last = mul(view, view, r)
                done(last)

            def gain(view, g, t, h, w):
                return mul(view, view, g.unsqueeze(1).unsqueeze(1).broadcast_to([128, t, h, w]))

            def heads(a, b, d=HD):
                return proj[:, :, a:b].rearrange("p t (h d) -> p t h d", d=d)

            def rope(x1, x2, c, s, a, b):
                mul(a, x2, s)
                done(mul(b, x1, s))
                mul(x1, x1, c)
                done(mul(x2, x2, c))
                V.tensor_tensor(x1, x1, a, ALU.subtract)
                return add(x2, x2, b)

            def prep(l, j):
                for i in range(1, len(PREP[j]), 2):
                    what, m = PREP[j][i]
                    dve.wait_ge(prep_full, l * N_PREP + prep_no(j, i) + 1)
                    dst, src = prep_target(j, what, m, i % 8)
                    V.tensor_copy(dst, src).then_inc(prep_copied[1], 1)

            def bias_and_max(l, it):
                j, maps, _, _ = ITEMS[it]
                g, hh = GROUPS[j], j % 2
                for m in maps:
                    q = j * MAPS + m
                    S, ns = scores(q), samples(g)
                    dve.wait_ge(scores_ready, l * N_MAPS + q + 1)
                    if g in "AB":
                        slope = (SLOPE_A[hh * 4 + m] if g == "A" else SLOPE_B[hh * 2 + m // 2]) / scale_of(g)
                        nd = T_NDA if g == "A" else T_NDB
                        for n, lo, hi, c in ((DSEQ, 0, ns, T_NDS + 576 - ns), (128, 576, 704, nd + 128), (128, 704, 960, nd)):
                            last = V.scalar_tensor_tensor(out=S[0:n, lo:hi], in0=table[0:n, c:c + hi - lo], scalar=slope,
                                                          in1=S[0:n, lo:hi], op0=ALU.mult, op1=ALU.add)
                        done(last)
                    else:
                        mask = table[:, T_MC:T_MC + 128] if g == "C" else table[:, T_MD:T_MD + 128]
                        if g == "D":
                            add(S[0:DSEQ, 512:576], S[0:DSEQ, 512:576], mask[0:DSEQ, 0:DSEQ])
                        add(S[:, 576:704], S[:, 576:704], mask)
                        done(add(S[:, 832:960], S[:, 832:960], mask))
                    for t, (lo, hi, n) in enumerate(((0, ns, DSEQ), (576, 704, 128), (704, 960, 128))):
                        last = V.tensor_reduce(mx[0:n, q, t:t + 1], S[0:n, lo:hi], X, ALU.max)
                    done(last)
                    if g == "A":
                        sink = v("a_sinks")[:, q:q + 1].broadcast_to([128, 3])
                        done(V.tensor_tensor(mx[:, q, :], mx[:, q, :], sink, ALU.max))
                        V.tensor_tensor(es[:, q, :], sink, mx[:, q, :], ALU.subtract).then_inc(sink_ready, 1)
                    V.tensor_scalar(sm[:, q, :], mx[:, q, :], -scale_of(g), None, ALU.mult).then_inc(shift_ready, 1)

            def attention(l, j):
                g, hh = GROUPS[j], j % 2
                its = [i for i, it in enumerate(ITEMS) if it[0] == j]
                bias_and_max(l, its[0])
                for it in its:
                    _, maps, col, w = ITEMS[it]
                    q = j * MAPS + maps[0]
                    if it + 1 in its:
                        bias_and_max(l, it + 1)
                    dve.wait_ge(probs_ready, l * N_MAPS + j * MAPS + maps[-1] + 1)
                    if g == "A":
                        done(add(sums[:, q, :], sums[:, q, :], es[:, q, :]))
                    done(V.reciprocal(rinv[:, q:q + len(maps), :], sums[:, q:q + len(maps), :]))
                    if g == "B":
                        done(V.tensor_scalar(rinv[:, q + 1, :], rinv[:, q + 1, :], lam[:, 5:6], None, ALU.mult))
                        P0, P1 = prob[:, q % 4, :], prob[:, q % 4 + 1, :]
                        spans = ((0, 576, DSEQ), (576, 704, 128), (704, 960, 128))
                        for t, (lo, hi, n) in enumerate(spans):
                            last = V.tensor_scalar(P1[0:n, lo:hi], P1[0:n, lo:hi], rinv[0:n, q + 1, t:t + 1], None, ALU.mult)
                        done(last)
                        for t, (lo, hi, n) in enumerate(spans):
                            last = V.scalar_tensor_tensor(out=P0[0:n, lo:hi], in0=P0[0:n, lo:hi], scalar=rinv[0:n, q, t:t + 1],
                                                          in1=P1[0:n, lo:hi], op0=ALU.mult, op1=ALU.subtract)
                        last.then_inc(mix_ready, 1)
                    dve.wait_ge(probsT_ready, l * N_ITEMS + it + 1)
                    if it:
                        dve.wait_ge(out_ready, l * N_ITEMS + it)
                    V.tensor_copy(probT[:, 0:384], ps[:, 4, 0:384]).then_inc(probT_copied[1], 1)
                    dve.wait_ge(out_ready, l * N_ITEMS + it + 1)
                    if it == its[0] and j:
                        dve.wait_ge(oT_full, l * 16 + 2 * j)
                    o = ps[:, 6, 0:3 * w].rearrange("p (t d) -> p t d", t=3)
                    if g == "B":
                        last = V.tensor_copy(otok[:, :, col:col + w], o)
                    else:
                        last = mul(otok[:, :, col:col + w], o, rinv[:, q, :].unsqueeze(2).broadcast_to([128, 3, w]))
                    if g == "B" or it != its[-1]:
                        last.then_inc(out_copied, 1)
                    else:
                        done(last)
                        V.tensor_copy(otmp[:, 0, 0:1], otok[:, 0, 0:1]).then_inc(out_copied, 1)
                if g == "B":
                    norm(l, f"O{j}")
                    gain(otok[:, :, :].rearrange("p t (h d) -> p t h d", d=128), v("b_gout"), 3, 2, 128).then_inc(job_out, 1)
                else:
                    V.tensor_copy(otmp[:, 0, 1:2], otok[:, 0, 0:1]).then_inc(job_out, 1)

            def block_done(l, n0, no, m, units=8):
                if m < 3:
                    dve.wait_ge(bank_full, l * 3 * CHUNKS + 3 * no + m + 1)
                else:
                    dve.wait_ge(unit_used, l * UNITS + n0 + units + RING)

            def add_chunk(l, n0, no, half, blk):
                for m in range(4):
                    block_done(l, n0, no, m)
                    d = x[:, blk + m, :] if isinstance(blk, int) else x[:, bass.ds(blk + m, 1), :]
                    s = ps[:, 4 * half + m, 0:TOK] if isinstance(blk, int) else ps[:, 4 * half + m:4 * half + m + 1, 0:TOK]
                    last = add(d, s, d)
                last.then_inc(half_free, 1)

            V.memset(ps[:, :, :], 0.0).then_inc(x_copied, 1)
            dve.sem_inc(job_out, 1)
            dve.wait_ge(cleared, 1)
            for k in range(KB):
                dve.wait_ge(x_full, k + 1)
                last = V.tensor_copy(x[:, k, :], ps[:, k % 8, 0:TOK])
                if k < KB - 1:
                    last.then_inc(x_copied, 1)
            last.then_inc(half_free, 2)
            dve.wait_ge(half_free, 2)
            with dve.Fori(0, DEPTH) as l:
                here[0] = l * STEPS
                count[0] = 0
                squares_pass(l, 0)
                w_in_chunks(l, "A")
                dve.wait_ge(vec_loaded, 16 * N_VEC * (l + 1))
                V.tensor_scalar(v("a_sinks"), v("a_sinks"), HD ** 0.5, None, ALU.mult)
                V.tensor_scalar(v("b_gout"), v("b_gout"), vec[:, VOFF["lam_init"] + 1:VOFF["lam_init"] + 2], None, ALU.mult)
                mul(otmp[:, 0, 0:HD], v("b_lq1"), v("b_lk1"))
                done(mul(otmp[:, 0, HD:2 * HD], v("b_lq2"), v("b_lk2")))
                V.tensor_reduce(lam[:, 0:2], otmp[:, 0, 0:2 * HD].rearrange("p (a d) -> p a d", a=2), X, ALU.add)\
                    .then_inc(lam_in, 1)
                norm(l, "A")
                gain(heads(0, 512), v("a_gq"), 3, 8, HD)
                gain(heads(512, 640), v("a_gk"), 3, 2, HD).then_inc(group_ready, 1)
                for j, g in enumerate(GROUPS):
                    if j == 2:
                        w_in_chunks(l, "B")
                        dve.wait_ge(lam_exp, l + 1)
                        done(V.tensor_tensor(lam[:, 4:5], lam[:, 2:3], lam[:, 3:4], ALU.subtract))
                        done(add(lam[:, 5:6], lam[:, 4:5], vec[:, VOFF["lam_init"]:VOFF["lam_init"] + 1]))
                        norm(l, "B")
                        gain(heads(0, 512), v("b_gq"), 3, 8, HD)
                        gain(heads(512, 1024), v("b_gk"), 3, 8, HD).then_inc(group_ready, 1)
                    if j == 4:
                        w_in_chunks(l, "C")
                        norm(l, "C")
                        mul(proj[:, :, 0:512], proj[:, :, 0:512],
                            vec[:, VOFF["c_gcq"]:VOFF["c_gcq"] + 512].unsqueeze(1).broadcast_to([128, 3, 512]))
                        done(mul(proj[:, :, 512:544], proj[:, :, 512:544],
                                 v("c_gkr").unsqueeze(1).broadcast_to([128, 3, ROPE])))
                        a = otmp[:, 0, 0:48].rearrange("p (t n) -> p t n", t=3)
                        b = otmp[:, 0, 48:96].rearrange("p (t n) -> p t n", t=3)
                        rope(proj[:, :, 512:528], proj[:, :, 528:544], cos, sin, a, b).then_inc(group_ready, 1)
                        z, az, e, u, d, ln, r = (fsm[:, i, :] for i in range(7))
                        done(add(z.rearrange("p (t h) -> p t h", t=3), proj[:, :, 544:552],
                                 v("d_bf").unsqueeze(1).broadcast_to([128, 3, 8])))
                        done(V.tensor_scalar(az, z, -1.0, None, ALU.mult))
                        V.tensor_tensor(az, az, z, ALU.max).then_inc(fz_ready, 1)
                        dve.wait_ge(fz_act, 2 * l + 1)
                        done(V.tensor_scalar(u, e, 1.0, None, ALU.add))
                        V.tensor_scalar(d, u, 1.0, 1e-30, ALU.subtract, ALU.add).then_inc(fz_ready, 1)
                        dve.wait_ge(fz_act, 2 * l + 2)
                        done(V.reciprocal(r, d))
                        done(V.tensor_scalar(ln, ln, 1e-30, None, ALU.add))
                        done(mul(r, r, ln))
                        done(mul(r, r, e))
                        dve.wait_ge(proj_free, l * 4 + 3)
                        zt, rt = z.rearrange("p (t h) -> p t h", t=3), r.rearrange("p (t h) -> p t h", t=3)
                        for o, i, n in ((5, 0, 2), (4, 2, 1)):
                            last = V.scalar_tensor_tensor(out=flog[:, o:o + n, :], in0=zt[:, i:i + n, :], scalar=0.0,
                                                          in1=rt[:, i:i + n, :], op0=ALU.min, op1=ALU.subtract)
                        last.then_inc(flog_ready, 1)
                        prep(l, "lat")
                    if g == "C":
                        hh = j - 4
                        for t in range(3):
                            if t < 2:
                                dve.wait_ge(lat_full, l * 16 + 8 * hh + t + 1)
                            else:
                                dve.wait_ge(unit_used, l * UNITS + LAT0 + 3 * hh + 2 + RING)
                            V.tensor_copy(qext[:, t, :, :], ps[:, t, 0:MAPS * CEXT].rearrange("p (m d) -> p m d", m=MAPS))\
                                .then_inc(lat_copied[1], 1)
                        for i in (1, 3, 5):
                            dve.wait_ge(lat_full, l * 16 + 8 * hh + 2 + i + 1)
                            b = 3 + i if i < 5 else i - 5
                            src = ps[:, b, :].rearrange("p (m d) -> p m d", m=MAPS)
                            V.tensor_copy(kext[:, i, :, 0:HD], src[:, :, 0:HD])
                            V.tensor_copy(vtok[:, i, :].rearrange("p (m d) -> p m d", m=MAPS), src[:, :, HD:128])\
                                .then_inc(lat_copied[1], 1)
                        norm(l, f"L{j}")
                        gain(kext[:, :, :, 0:HD], v("c_gkn"), 7, MAPS, HD)
                        done(gain(qext[:, :, :, :], vec[:, VOFF["c_gqn"]:VOFF["c_gqn"] + CEXT], 3, MAPS, CEXT))
                        a = otmp[:, 0, 0:192].rearrange("p (t m n) -> p t m n", t=3, m=MAPS)
                        b = otmp[:, 1, 0:192].rearrange("p (t m n) -> p t m n", t=3, m=MAPS)
                        c4 = cos.unsqueeze(2).broadcast_to([128, 3, MAPS, 16])
                        s4 = sin.unsqueeze(2).broadcast_to([128, 3, MAPS, 16])
                        rope(qext[:, :, :, HD:HD + 16], qext[:, :, :, HD + 16:CEXT], c4, s4, a, b)
                        dve.wait_ge(kc_loaded, 16 * (l * KC[-1] + KC[4]))
                        V.tensor_copy(kext[:, 0:4, :, HD:CEXT],
                                      kcache[:, 0:4, CKVR:CKVR + ROPE].unsqueeze(2).broadcast_to([128, 4, MAPS, ROPE]))
                        V.tensor_copy(kext[:, 4:5, :, HD:CEXT],
                                      proj[:, 2:3, 512:544].unsqueeze(2).broadcast_to([128, 1, MAPS, ROPE]))
                        V.tensor_copy(kext[:, 5:7, :, HD:CEXT],
                                      proj[:, 0:2, 512:544].unsqueeze(2).broadcast_to([128, 2, MAPS, ROPE]))\
                            .then_inc(ext_ready, 1)
                    if j == 6:
                        w_in_chunks(l, "D")
                        norm(l, "D")
                        gain(heads(0, 512), v("d_gq"), 3, 8, HD)
                        gain(heads(512, 1024), v("d_gk"), 3, 8, HD).then_inc(group_ready, 1)
                        dve.wait_ge(group_ready, 4 * l + 4)
                        dve.wait_ge(fcum_full, l + 1)
                        done(V.tensor_copy(fcum[:, :, :], ps[:, 0, 0:56].rearrange("p (t h) -> p t h", t=7)))
                    if g == "D":
                        hh = j % 2
                        K, Q = kext_of("D"), qext_of("D")
                        dve.wait_ge(kc_loaded, 16 * (l * KC[-1] + KC[j]))
                        if hh:
                            dve.wait_ge(job_out, l * 8 + j + 1)
                        sel = slice(hh * 4, hh * 4 + 4)
                        V.tensor_copy(K[:, 0:4, :, 0:HD], kcache[:, :, :].rearrange("p t (m d) -> p t m d", m=MAPS))
                        nk = proj[:, :, 512 + hh * 256:768 + hh * 256].rearrange("p t (m d) -> p t m d", m=MAPS)
                        nq = proj[:, :, hh * 256:(hh + 1) * 256].rearrange("p t (m d) -> p t m d", m=MAPS)
                        V.tensor_copy(K[:, 4:5, :, 0:HD], nk[:, 2:3, :, :])
                        V.tensor_copy(K[:, 5:7, :, 0:HD], nk[:, 0:2, :, :])
                        V.tensor_copy(Q[:, :, :, 0:HD], nq)
                        V.tensor_scalar(K[:, :, :, HD], fcum[:, :, sel], -(HD ** 0.5), None, ALU.mult)
                        V.memset(K[:, :, :, HD + 1], 1.0)
                        V.memset(Q[:, :, :, HD], 1.0)
                        V.tensor_scalar(Q[:, 0:2, :, HD + 1], fcum[:, 5:7, sel], HD ** 0.5, None, ALU.mult)
                        V.tensor_scalar(Q[:, 2:3, :, HD + 1], fcum[:, 4:5, sel], HD ** 0.5, None, ALU.mult)\
                            .then_inc(ext_ready, 1)
                    prep(l, j)
                    attention(l, j)
                assert count[0] < STEPS - 40
                dve.wait_ge(hid_copied, (l + 1) * 16)
                for b in range(0, KB, 4):
                    done(V.tensor_copy(htmp[:, b // 4 % 2, :, :], hid[:, b:b + 4, :]))
                    done(V.tensor_tensor(hlo[:, b:b + 4, :], hid[:, b:b + 4, :], htmp[:, b // 4 % 2, :, :].bitcast(f32), ALU.subtract))
                    V.tensor_copy(hhi[:, b:b + 4, :], htmp[:, b // 4 % 2, :, :].bitcast(f32)).then_inc(split_ready, 4)
                with dve.Fori(0, 2) as c2:
                    for h in range(2):
                        add_chunk(l, TAIL0 + 16 * c2 + 8 * h, c2 * 2 + h, h, c2 * 8 + h * 4)
                gain_split(l, 1, 4)
                squares_pass(l, 4)
                UP_STEPS = 2 * KB - 4
                with dve.Fori(0, FG) as g:
                    here[0] = l * STEPS + g * UP_STEPS
                    at0 = count[0]
                    dve.wait_ge(rms_ready, l * N_RMS + g + 2)
                    V.reciprocal(rfeat[:, :], rroot[:, :]).then_inc(inv_ready, 1)
                    dve.wait_ge(inv_ready, l * (FG + 1) + g + 1)
                    for c in range(4):
                        for m in range(4):
                            block_done(l, TAIL0 + 32 + 64 * g + 8 * c, 4 + 8 * g + c, m)
                            ins = V.scalar_tensor_tensor(out=t0[:, m % 2, :], in0=ps[:, 4 * (c % 2) + m, 0:TOK], scalar=0.0,
                                                         in1=rfeat[:, :], op0=ALU.max, op1=ALU.mult)
                            if m < 3:
                                done(ins)
                            else:
                                ins.then_inc(half_free, 1)
                                dve.wait_ge(half_free, l * CHUNKS + 2 + 4 + 8 * g + c + 1)
                            mul(hhi[:, 4 * c + m, :], t0[:, m % 2, :], t0[:, m % 2, :])
                            done(mul(t1[:, m % 2, :], t0[:, m % 2, :], t0[:, m % 2, :]))
                            V.tensor_tensor(hlo[:, 4 * c + m, :], t1[:, m % 2, :], hhi[:, 4 * c + m, :].bitcast(f32),
                                            ALU.subtract).then_inc(hid_ready, 1)
                    assert count[0] - at0 == UP_STEPS
                    for c in range(4):
                        add_chunk(l, TAIL0 + 64 + 64 * g + 8 * c, 8 + 8 * g + c, c % 2, 4 * c)
                here[0] = l * STEPS
                count[0] += (FG - 1) * UP_STEPS
                dve.wait_ge(pleT_full, l + 1)
                done(V.tensor_copy(pleh[:, :, :], ps[:, 4:6, 0:TOK]))
                V.tensor_tensor(plel[:, :, :], ps[:, 4:6, 0:TOK], pleh[:, :, :].bitcast(f32), ALU.subtract)\
                    .then_inc(pleT_copied, 1)
                gain_split(l, 2, 4 + 8 * FG)
                for c in range(4):
                    for m in range(4):
                        block_done(l, TAIL0 + 288 + c, 36 + c, m, 1)
                        last = V.tensor_copy(plout[:, 4 * c + m, :], ps[:, 4 * (c % 2) + m, 0:TOK])
                    last.then_inc(half_free, 1)
                squares_pass(l, 4 + 8 * FG)
                dve.wait_ge(rms_ready, l * N_RMS + N_RMS)
                V.reciprocal(rfeat[:, :], rroot[:, :]).then_inc(inv_ready, 1)
                dve.wait_ge(inv_ready, (l + 1) * (FG + 1))

                def finish(b):
                    dve.wait_ge(sig_ready, l * 16 + b + 1)
                    done(mul(plout[:, b, :], t1[:, b % 2, :], plout[:, b, :]))
                    last = add(x[:, b, :], x[:, b, :], plout[:, b, :])
                    if b % 4 == 3:
                        last.then_inc(half_free, 1)

                for b in range(KB):
                    c, m = b // 4, b % 4
                    if b and m == 0:
                        finish(b - 1)
                    block_done(l, TAIL0 + 292 + 8 * c, 40 + c, m)
                    mul(t0[:, b % 2, :], ps[:, 4 * (c % 2) + m, 0:TOK], rfeat[:, :]).then_inc(sig_in, 1)
                    if m:
                        finish(b - 1)
                finish(KB - 1)
                V.memset(lam[:, 7:8], 0.0).then_inc(step, STEPS - count[0])
                dve.wait_ge(half_free, (l + 1) * CHUNKS + 2)
            hflat = hid[:, :, :].rearrange("p a b -> p (a b)")
            for i in range(12):
                t, q = i // 4, i % 4
                n = 128 if t < 2 else DSEQ
                dve.wait_ge(y_full, i + 1)
                dst = hflat[:, t * DM + q * 512:t * DM + (q + 1) * 512] if t < 2 else arena[0:DSEQ, q * 512:(q + 1) * 512]
                V.tensor_copy(dst, ps[0:n, i % 8, :]).then_inc(y_copied, 1)


OUTS = [("y_prompt", (1, SEQ, DM)), ("y_sample", (1, DSEQ, DM)),
        ("a_k_p", (DEPTH, 1, WINDOW, 2, HD)), ("a_v_p", (DEPTH, 1, WINDOW, 2, HD)),
        ("b_k_p", (DEPTH, 1, SEQ, 4, 2, HD)), ("b_v_p", (DEPTH, 1, SEQ, 4, 128)),
        ("c_kv_p", (DEPTH, 1, SEQ, CKVR)), ("c_krope_p", (DEPTH, 1, SEQ, ROPE)),
        ("d_k_p", (DEPTH, 1, SEQ, 8, HD)), ("d_v_p", (DEPTH, 1, SEQ, 8, HD)), ("d_logf_p", (DEPTH, 1, SEQ, 8)),
        ("a_k_s", (DEPTH, 1, WINDOW, 2, HD)), ("a_v_s", (DEPTH, 1, WINDOW, 2, HD)),
        ("b_k_s", (DEPTH, 1, DSEQ, 4, 2, HD)), ("b_v_s", (DEPTH, 1, DSEQ, 4, 128)),
        ("c_kv_s", (DEPTH, 1, DSEQ, CKVR)), ("c_krope_s", (DEPTH, 1, DSEQ, ROPE)),
        ("d_k_s", (DEPTH, 1, DSEQ, 8, HD)), ("d_v_s", (DEPTH, 1, DSEQ, 8, HD)), ("d_logf_s", (DEPTH, 1, DSEQ, 8))]


def constants():
    import math
    import numpy as np
    t = np.zeros((128, T_END), np.float32)
    p = np.arange(128)
    t[:, T_ID:T_ID + 128] = np.eye(128)
    t[:, T_TRI:T_TRI + 128] = p[:, None] <= p[None, :]
    q, k = 128 + p[:, None], np.arange(256)[None, :]
    dist = -np.abs(q - k).astype(np.float32)
    qc, kc = q // CHUNK, k // CHUNK
    t[:, T_NDA:T_NDA + 256] = np.where((kc <= qc) & (kc >= qc - WINDOW // CHUNK), dist, NEG)
    t[:, T_NDB:T_NDB + 256] = np.where(kc <= qc, dist, NEG)
    t[:, T_MC:T_MC + 128] = np.where(p[None, :] // CHUNK <= p[:, None] // CHUNK, 0, NEG)
    t[:, T_MD:T_MD + 128] = np.where(p[None, :] <= p[:, None], 0, NEG)
    t[:, T_NDS:T_NDS + KEYS] = -np.abs(PAST + p[:, None] - np.arange(KEYS)[None, :])
    half = ROPE // 2
    inv = np.float32(10000.0) ** (-np.arange(half, dtype=np.float32) / np.float32(half))
    for tile, first in enumerate((0, 128, PAST)):
        ang = ((first + p).astype(np.float32)[:, None] * inv).astype(np.float32)
        t[:, T_COS + 16 * tile:T_COS + 16 * (tile + 1)] = np.cos(ang)
        t[:, T_SIN + 16 * tile:T_SIN + 16 * (tile + 1)] = np.sin(ang)
    lam = [0.8 - 0.6 * math.exp(-0.3 * li) for li in range(DEPTH)]
    return {"table": t, "lam_init": np.array([[v, 1.0 - v] for v in lam], np.float32)}


def kernel(**inputs):
    import numpy as np
    import concourse.bacc as bacc
    from concourse.bass_utils import run_bass_kernel_spmd

    nc = bacc.Bacc("TRN2", target_bir_lowering=False, num_devices=1)
    arrays, I, O = {}, {}, {}
    for name, a in {**inputs, **constants()}.items():
        a = np.ascontiguousarray(a)
        arrays[f"in_{name}"] = a
        I[name] = nc.dram_tensor(f"in_{name}", a.shape, mybir.dt.from_np(a.dtype), kind="ExternalInput").ap()
    for name, shape in OUTS:
        O[name] = nc.dram_tensor(f"out_{name}", shape, mybir.dt.float32, kind="ExternalOutput").ap()
    build(nc, I, O)
    r = run_bass_kernel_spmd(nc, [arrays], core_ids=[0])
    return tuple(r.results[0][f"out_{name}"] for name, _ in OUTS)
```

```python
import concourse.bass as bass
from concourse import mybir
from contextlib import ExitStack

DM, SEQ, DSEQ, PAST, DEPTH = 2048, 256, 64, 512, 2
TOK = SEQ + DSEQ
CHUNK, WINDOW = 64, 128
HD = 64
ROPE, CQR, CKVR = 32, 384, 128
FF, PLE = 8192, 256
EPS = 1e-6
NEG = -1e30
KB = DM // 128
UK = 2
RING = 4
FG = FF // DM
W_A, W_B, W_C, W_D = 0, 768, 2304, 2848
CEXT, DEXT = HD + ROPE, HD + 2
KEYS = PAST + DSEQ
ALLK = KEYS + SEQ

T_ID, T_TRI, T_NDA, T_NDB, T_MC, T_MD, T_NDS, T_COS, T_SIN, T_END = (
    0, 128, 256, 512, 768, 896, 1024, 1600, 1648, 1696)

VECS = [("a_gq", HD), ("a_gk", HD), ("b_gq", HD), ("b_gk", HD), ("d_gq", HD), ("d_gk", HD), ("c_gcq", CQR),
        ("c_gckv", CKVR), ("c_gkr", ROPE), ("c_gqn", HD), ("c_gqr", ROPE), ("c_gkn", HD), ("b_gout", 128),
        ("a_sinks", 8), ("d_bf", 8), ("b_lq1", HD), ("b_lk1", HD), ("b_lq2", HD), ("b_lk2", HD), ("lam_init", 2)]
VOFF, _n = {}, 0
for _name, _w in VECS:
    VOFF[_name] = _n
    _n += _w
VW = _n

GROUPS = "AABBCCDD"
MAPS = 4


def items_of(group):
    return [((0, 1), 0, 128), ((2, 3), 128, 128)] if group == "B" else [((m,), m * HD, HD) for m in range(MAPS)]


ITEMS = [(j, maps, col, w) for j, g in enumerate(GROUPS) for maps, col, w in items_of(g)]
N_ITEMS = len(ITEMS)
N_MAPS = MAPS * len(GROUPS)


def build(nc, I, O):
    f32 = mybir.dt.float32
    ALU, ACT, AX = mybir.AluOpType, mybir.ActivationFunctionType, mybir.AxisListType
    X = AX.X
    ctx = ExitStack()
    with ctx:
        f32r = mybir.dt.float32r
        top = [nc.sbuf_base + (-nc.sbuf_base) % 64]

        def sb(name, shape, dtype=f32, at=None):
            words = 1
            for n in shape[1:]:
                words *= n
            if at is None:
                at = top[0]
                top[0] += 4 * (words + (-words) % 8)
            return nc.alloc_sbuf_tensor_at(name, shape, dtype, offset=at)

        def sem(name):
            return ctx.enter_context(nc.semaphore(name))

        x = sb("x", [128, KB, TOK])
        at = top[0]
        xg = sb("xg", [128, KB * TOK + 64])
        xhi = sb("xhi", [128, KB, TOK], f32r, at)
        at = top[0]
        hid = sb("hid", [128, KB, TOK])
        hhi = sb("hhi", [128, KB, TOK], f32r, at)
        ring = sb("ring", [128, RING, 1024])
        table = sb("table", [128, T_END])
        vec = sb("vec", [128, VW])
        gains = sb("gains", [128, 3, KB])
        ones = sb("ones", [128, 128])
        eps = sb("eps", [128, 1])
        arena = sb("arena", [128, KB * TOK])
        proj_bd = arena[:, 0:3 * 1544].rearrange("p (t n) -> p t n", t=3)
        plout = arena[:, :].rearrange("p (b n) -> p b n", b=KB)
        otok = sb("otok", [128, 3, 256])
        otmp = sb("otmp", [128, 3, 256])
        flog = sb("flog", [128, 7, 8])
        fcum = sb("fcum", [128, 7, 8])
        fsm = sb("fsm", [128, 8, 24])
        mx = sb("mx", [128, N_MAPS, 3])
        sums = sb("sums", [128, N_MAPS, 3])
        sm = sb("sm", [128, N_MAPS, 3])
        es = sb("es", [128, 8, 3])
        rinv = sb("rinv", [128, N_MAPS, 3])
        ssq = sb("ssq", [128, 64])
        root = sb("root", [128, 64])
        rstd = sb("rstd", [128, 64])
        lam = sb("lam", [128, 8])
        rtok = sb("rtok", [128, 3])
        rroot = sb("rroot", [128, TOK])
        rfeat = sb("rfeat", [128, TOK])
        acc = sb("acc", [128, TOK + 64])
        at = top[0]
        proj_ac = sb("proj_ac", [128, 3, 768], at=at)
        t0 = sb("t0", [128, 2, TOK])
        t1 = sb("t1", [128, 2, TOK])
        pleh = sb("pleh", [128, 2, TOK], f32r)
        plel = sb("plel", [128, 2, TOK], f32r)
        region = top[0]
        cqT = sb("cqT", [128, 3 * TOK + 64])
        ckvT = sb("ckvT", [128, ALLK])
        kT = sb("kT", [128, MAPS, ALLK])
        qT = sb("qT", [128, MAPS, TOK])
        kext = sb("kext", [128, 7, MAPS, CEXT])
        qext = sb("qext", [128, 3, MAPS, CEXT])
        vtok = sb("vtok", [128, 7, 256])
        kcache = sb("kcache", [128, 4, 256])
        prob = sb("prob", [128, 4, 960])
        probT = sb("probT", [128, 704])
        end, top[0] = top[0], region
        cqT_pad = cqT[:, 3 * TOK:]
        whi = sb("whi", [128, RING, 1024], f32r)
        wlo = sb("wlo", [128, RING, 1024], f32r)
        at = top[0]
        xlo = sb("xlo", [128, KB, TOK], f32r)
        htmp = sb("htmp", [128, 4, TOK], f32r, at)
        hlo = sb("hlo", [128, KB, TOK], f32r)
        assert max(end, top[0]) <= nc.sbuf_usable_end
        sq = prob[:, :, :].rearrange("p a b -> p (a b)")
        ps = ctx.enter_context(nc.psum_tensor("ps", [128, 8, 512], f32))
        psf = ps[:, :, :].rearrange("p b n -> p (b n)")

        ident = table[:, T_ID:T_ID + 128]
        tri = table[:, T_TRI:T_TRI + 128]
        cos = table[:, T_COS:T_COS + 48].rearrange("p (t n) -> p t n", t=3)
        sin = table[:, T_SIN:T_SIN + 48].rearrange("p (t n) -> p t n", t=3)

        def proj(g):
            return proj_ac if g in "AC" else proj_bd

        def v(name):
            w = dict(VECS)[name]
            return vec[:, VOFF[name]:VOFF[name] + w]

        raw_loaded = [sem(f"raw_loaded{i}") for i in range(RING)]
        unit_used = sem("unit_used")
        bank_full = sem("bank_full")
        half_free = sem("half_free")
        wout_full = sem("wout_full")
        wout_added = sem("wout_added")
        hid_ready = sem("hid_ready")
        gained = sem("gained")
        split_ready = sem("split_ready")
        hi_ready = sem("hi_ready")
        lo_ready = sem("lo_ready")
        acc_ready = sem("acc_ready")
        rms_summed = sem("rms_summed")
        rms_ready = sem("rms_ready")
        inv_ready = sem("inv_ready")
        sig_in = sem("sig_in")
        sig_ready = sem("sig_ready")
        proj_full = sem("proj_full")
        proj_copied = sem("proj_copied")
        sq_ready = sem("sq_ready")
        ssq_ready = sem("ssq_ready")
        root_ready = sem("root_ready")
        group_ready = sem("group_ready")
        prep_full = sem("prep_full")
        prep_copied = [sem("prep_copied_act"), sem("prep_copied_dve")]
        ext_ready = sem("ext_ready")
        lat_full = sem("lat_full")
        lat_copied = [sem("lat_copied_act"), sem("lat_copied_dve")]
        fz_ready = sem("fz_ready")
        fz_act = sem("fz_act")
        flog_ready = sem("flog_ready")
        fcum_full = sem("fcum_full")
        lam_in = sem("lam_in")
        lam_exp = sem("lam_exp")
        scores_ready = sem("scores_ready")
        shift_ready = sem("shift_ready")
        probs_ready = sem("probs_ready")
        sink_ready = sem("sink_ready")
        mix_ready = sem("mix_ready")
        probsT_ready = sem("probsT_ready")
        probT_copied = [sem("probT_copied_act"), sem("probT_copied_dve")]
        out_ready = sem("out_ready")
        out_copied = sem("out_copied")
        job_out = sem("job_out")
        oT_full = sem("oT_full")
        hid_copied = sem("hid_copied")
        mix_loaded = sem("mix_loaded")
        vec_loaded = sem("vec_loaded")
        kc_loaded = sem("kc_loaded")
        vc_loaded = sem("vc_loaded")
        fc_loaded = sem("fc_loaded")
        ple_loaded = sem("ple_loaded")
        pleT_full = sem("pleT_full")
        pleT_copied = sem("pleT_copied")
        stored = sem("stored")
        proj_free = sem("proj_free")
        table_loaded = sem("table_loaded")
        x_loaded = sem("x_loaded")
        x_full = sem("x_full")
        x_copied = sem("x_copied")
        y_full = sem("y_full")
        y_copied = sem("y_copied")
        pad_cleared = sem("pad_cleared")
        cleared = sem("cleared")
        pe_passed = sem("pe_passed")
        pool_passed = sem("pool_passed")
        step = sem("dve_step")

        block = ctx.enter_context(nc.Block())

        UNITS, TAIL0 = 408, 108
        TAIL = UNITS - TAIL0
        MLP0 = TAIL0 + 8
        Q_MLP, Q_PLE = MLP0 // RING, MLP0 // RING + 16 * FG
        SLOT = UNITS // RING
        CHUNKS = 44
        N_RMS = 2 + FG
        SLOPE_A = [2.0 ** -(h + 1) for h in range(8)]
        SLOPE_B = [2.0 ** -(2 * (h + 1)) for h in range(4)]
        WIN = {"A": [(0, 8, 2, 512, 0), (1, 4, 4, 256, 512)],
               "B": [(2, 8, 2, 512, 0), (3, 8, 2, 512, 512), (4, 8, 2, 512, 1024)],
               "C": [(5, 4, 4, 256, 0), (6, 8, 2, 288, 256)],
               "D": [(7, 8, 2, 512, 0), (8, 8, 2, 512, 512), (9, 8, 2, 264, 1024), (10, 4, 4, 256, 1288)]}
        CHUNK_AT = {c[0]: c for cs in WIN.values() for c in cs}
        N_WIN = len(CHUNK_AT)
        FILL = {0: {"prep": 6, "copied": 1, "T0": 7, "V0": 1, "T1": 9, "T2": 8, "V2": 1, "T3": 5, "V3": 1, "out": 1},
                1: {"prep": 3, "copied": 1, "T0": 4, "T1": 7, "V1": 1, "T2": 6, "V2": 1, "T3": 6, "V3": 1, "out": 2},
                2: {"prep": 8, "copied": 1, "S0": 3, "T0": 8, "V0": 2, "T1": 9, "V1": 1, "out": 4},
                4: {"norm": 6, "lat": 10, "copied": 1, "T0": 4, "V0": 1, "T1": 2, "T2": 5, "V2": 1, "T3": 4, "V3": 1, "out": 1},
                5: {"lat": 10, "copied": 1, "T0": 1, "T1": 10, "V1": 2, "T2": 10, "V2": 2, "T3": 7, "V3": 1, "out": 4}}

        OUT_K = [(0, 4), (4, 12)]
        OUT_PARTS = (1, 2)
        OUT_FILL = {3: {"prep": 3, "copied": 1, "S0": 2, "T0": 2, "V0": 1, "T1": 3, "V1": 1, "out": 3},
                    6: {"norm": 6, "prep": 1, "copied": 1, "T0": 2, "V0": 1, "T1": 2, "V1": 1, "T2": 2, "V2": 1, "T3": 2, "V3": 1},
                    7: {"prep": 1, "T0": 2, "V0": 1, "T1": 2, "V1": 1, "T2": 2, "V2": 1, "T3": 2}}

        def pieces(g):
            return [(no, u, t) for no, units, _, _, _ in WIN[g] for u in range(units) for t in range(3)]

        AT = {}
        STREAM = [(no, u) for no, u, t in pieces("A") if t == 0]
        for _g, _next in ("AB", "BC", "CD"):
            _todo = pieces(_next)
            for _j in [j for j, g in enumerate(GROUPS) if g == _g and j in FILL]:
                for _place, _n in FILL[_j].items():
                    if _place == "lat":
                        STREAM += [("lat", 4 * (_j - 4) + i) for i in range(4)]
                    AT[_j, _place], _todo = _todo[:_n], _todo[_n:]
                    STREAM += [(no, u) for no, u, t in AT[_j, _place] if t == 0]
                    assert all(x[0] == y[0] for x, y in zip(AT[_j, _place], AT[_j, _place][1:]))
            assert not _todo
            if _g == "B":
                STREAM += [("out0", i) for i in range(KB // 2)]
        STREAM += [("out1", i) for i in range(KB)]
        OUT_AT = {}
        for _round, _jobs in enumerate(((3,), (6, 7))):
            _n = 0
            for _j in _jobs:
                for _place, _w in OUT_FILL[_j].items():
                    _parts = OUT_PARTS[_round]
                    OUT_AT[_j, _place] = [(_round, (_n + i) // _parts, (_n + i) % _parts) for i in range(_w)]
                    _n += _w
            assert _n == KB * _parts
        assert len(STREAM) == TAIL0
        POS = {unit: i for i, unit in enumerate(STREAM)}

        def out_bank(b):
            return 5 + b % 3

        def chunk_bank(no):
            return 0 if no == 1 else 5

        NORM = {n: i for i, n in enumerate(["A", "B", "O2", "O3", "C", "L4", "L5", "D"])}
        N_NORM = len(NORM)
        PREP = {}
        for j, g in enumerate(GROUPS):
            PREP[j] = [("q", m) for m in range(MAPS)]
            PREP[j] += [(k, m) for m in (range(1) if g == "A" else range(MAPS)) for k in ("kc", "kn")]
            if j == 4:
                PREP["lat"] = [("cq", 0), ("cq", 1), ("cq", 2), ("ckvc", 0), ("ckvn", 0)]
        ORDER = [0, 1, 2, 3, "lat", 4, 5, 6, 7]
        PREP_BASE, _t = {}, [0, 0]
        for j in ORDER:
            PREP_BASE[j] = tuple(_t)
            n = len(PREP[j])
            _t = [_t[0] + (n + 1) // 2, _t[1] + n // 2]
        PREP_TOT = tuple(_t)
        N_PREP = sum(_t)
        KEXTENT = {"A": HD, "B": HD, "C": CEXT, "D": DEXT}

        def prep_no(j, i):
            return sum(PREP_BASE[j]) + i

        def prep_waits(l, j, n):
            return (l * PREP_TOT[0] + PREP_BASE[j][0] + (n + 1) // 2, l * PREP_TOT[1] + PREP_BASE[j][1] + n // 2)

        def scores(q):
            return psf[:, (q % 2) * 1024:(q % 2) * 1024 + 960]

        def transposed(it):
            b = 2 * (ITEMS[it][1][-1] % 2)
            return ps[:, b, :], ps[:, b + 1, :]

        def lat_bank(i):
            return (3 + i) % 5

        def cached_keys(g):
            return WINDOW if g == "A" else PAST

        def samples(g):
            return cached_keys(g) + DSEQ

        def kdT(j):
            return kT[0:KEXTENT[GROUPS[j]], :, :]

        def kext_of(g):
            w = KEXTENT[g]
            return kext[:, :, :, :].rearrange("p a b c -> p (a b c)")[:, 0:7 * MAPS * w].rearrange(
                "p (t m c) -> p t m c", t=7, m=MAPS)

        def qext_of(g):
            w = KEXTENT[g]
            return qext[:, :, :, :].rearrange("p a b c -> p (a b c)")[:, 0:3 * MAPS * w].rearrange(
                "p (t m c) -> p t m c", t=3, m=MAPS)

        def query_src(j, m, t):
            g, hh = GROUPS[j], j % 2
            if g in "AB":
                return proj(g)[:, t, hh * 256 + m * HD:hh * 256 + (m + 1) * HD]
            return qext_of(g)[:, t, m, :]

        def new_key_src(j, m, t):
            g, hh = GROUPS[j], j % 2
            if g == "A":
                return proj(g)[:, t, 512 + hh * HD:512 + (hh + 1) * HD]
            if g == "B":
                return proj(g)[:, t, 512 + hh * 256 + m * HD:512 + hh * 256 + (m + 1) * HD]
            return kext_of(g)[:, (5, 6, 4)[t], m, :]

        def cached_key_src(j, m, t):
            g = GROUPS[j]
            return kcache[:, t, m * HD:(m + 1) * HD] if g in "AB" else kext_of(g)[:, t, m, :]

        def values(j, col, w, t):
            g, hh = GROUPS[j], j % 2
            if g == "C":
                return vtok[:, t, col:col + w]
            if t < 4:
                return vtok[:, t, 0:HD] if g == "A" else vtok[:, t, col:col + w]
            tile = {4: 2, 5: 0, 6: 1}[t]
            if g == "A":
                return proj(g)[:, tile, 640 + hh * HD:640 + (hh + 1) * HD]
            return proj(g)[:, tile, 1024 + hh * 256 + col:1024 + hh * 256 + col + w]

        @block.sync
        def _(sp):
            def load(l, q4, u, dst_cols, src, tail=False):
                s = u % RING
                if tail:
                    sp.wait_ge(lo_ready, l * TAIL + 4 * q4 + u + 1 - TAIL0 - RING)
                else:
                    sp.wait_ge(unit_used, l * UNITS + 4 * q4 + u + 1)
                dst = ring[:, s, 0:dst_cols]
                if len(src.shape) == 3:
                    dst = dst.rearrange("p (a n) -> p a n", a=src.shape[1])
                sp.dma_start(dst, src).then_inc(raw_loaded[s], 16)

            def chunk(l, q4, w, rows, cols, ncol, kb):
                for u in range(KB // kb):
                    src = w[l, bass.ds(rows + u * kb * 128, kb * 128), bass.ds(cols, ncol)]
                    load(l, q4, u, kb * ncol, src.rearrange("(a p) n -> p a n", p=128), True)

            for tile in range(2):
                sp.dma_start(hid[:, :, :].rearrange("p a b -> p (a b)")[:, tile * DM:(tile + 1) * DM],
                             I["x_prompt"][0, tile * 128:(tile + 1) * 128, :]).then_inc(x_loaded, 16)
            sp.dma_start(arena[0:DSEQ, 0:DM], I["x_sample"][0, :, :]).then_inc(x_loaded, 16)
            with sp.Fori(0, DEPTH) as l:
                for i, (no, u) in enumerate(STREAM):
                    if no == "lat":
                        hh, part = u // 4, u % 4
                        src = (I["c_wq_up"][l, part * 128:(part + 1) * 128, hh * 384:(hh + 1) * 384] if part < 3
                               else I["c_wkv_up"][l, :, hh * 512:(hh + 1) * 512])
                        load(l, i // RING, i % RING, src.shape[1], src)
                        continue
                    if no in ("out0", "out1"):
                        (k0, k1), n = OUT_K[int(no[3])], (256, 128)[int(no[3])]
                        load(l, i // RING, i % RING, (k1 - k0) * n,
                             I["w_out"][l, k0 * 128:k1 * 128, u * n:(u + 1) * n].rearrange("(a p) n -> p a n", p=128))
                        continue
                    _, _, nk, ncol, c0 = CHUNK_AT[no]
                    first = {"A": W_A, "B": W_B, "C": W_C, "D": W_D}[[g for g in WIN if CHUNK_AT[no] in WIN[g]][0]]
                    cols, rows = (first + c0, ncol), (u * nk * 128, nk * 128)
                    src = I["w_in"][l, rows[0]:rows[0] + rows[1], cols[0]:cols[0] + cols[1]]
                    load(l, i // RING, i % RING, nk * cols[1], src.rearrange("(a p) n -> p a n", p=128))
                for c in range(4):
                    for u in range(2):
                        n, k = 2 * c + u, OUT_K[1][1] + 2 * u
                        load(l, (TAIL0 + n) // RING, n % RING, 1024,
                             I["w_out"][l, k * 128:(k + 2) * 128, 512 * c:512 * (c + 1)].rearrange("(a p) n -> p a n", p=128),
                             n >= RING)
                with sp.Fori(0, FG) as g:
                    with sp.Fori(0, 4) as c:
                        chunk(l, Q_MLP + 16 * g + 2 * c, I["w_up"], 0, DM * g + 512 * c, 512, 2)
                    with sp.Fori(0, 4) as c:
                        chunk(l, Q_MLP + 8 + 16 * g + 2 * c, I["w_down"], DM * g, 512 * c, 512, 2)
                for c in range(4):
                    load(l, Q_PLE, c, 1024, I["w_ple"][l, :, 512 * c:512 * (c + 1)].rearrange("(a p) n -> p a n", p=128),
                         True)
                with sp.Fori(0, 4) as c:
                    chunk(l, Q_PLE + 1 + 2 * c, I["w_ple_gate"], 0, 512 * c, 512, 2)
            for tile in range(2):
                sp.wait_ge(y_copied, 4 * (tile + 1))
                sp.dma_start(O["y_prompt"][0, tile * 128:(tile + 1) * 128, :],
                             hid[:, :, :].rearrange("p a b -> p (a b)")[:, tile * DM:(tile + 1) * DM]).then_inc(x_loaded, 16)
            sp.wait_ge(y_copied, 12)
            sp.dma_start(O["y_sample"][0, :, :], arena[0:DSEQ, 0:DM]).then_inc(x_loaded, 16)
            sp.wait_ge(x_loaded, 96)

        STORED = (6, 10, 14, 20)
        N_STORED = STORED[-1]

        @block.gpsimd
        def _(pool):
            def hold(s, value):
                pool.wait_ge(s, value)
                pool.sem_inc(pool_passed, 1)

            pool.dma_start(table[:, :], I["table"]).then_inc(table_loaded, 16)
            pool.sem_inc(proj_free, 1)
            for t, val in ((ones[:, :], 1.0), (eps[:, :], EPS), (xg[:, KB * TOK:], 0.0),
                           (acc[:, TOK:], 0.0), (mx[:, :, :], 0.0), (flog[:, :, :], 0.0)):
                nc.gpsimd.memset(t, val)
            nc.gpsimd.memset(sums[:, :, :], 1.0).then_inc(cleared, 1)
            with pool.Fori(0, DEPTH) as l:
                hold(job_out, l * 8 + 1)
                with nc.allow_non_contiguous_dma("feature-major gains"):
                    pool.dma_start(gains[:, 0, :], I["g_mix"][l, :].rearrange("(a p) -> p a", p=128)).then_inc(mix_loaded, 16)
                hold(half_free, l * CHUNKS + 2)
                nc.gpsimd.memset(cqT_pad, 0.0).then_inc(pad_cleared, 1)
                for name, w in VECS:
                    src = I[name][l, :] if name != "lam_init" else I["lam_init"][l, :]
                    pool.dma_start(vec[:, VOFF[name]:VOFF[name] + w], src.partition_broadcast(128)).then_inc(vec_loaded, 16)
                with nc.allow_non_contiguous_dma("feature-major gains"):
                    for i, name in enumerate(("g_mlp", "g_ple")):
                        pool.dma_start(gains[:, 1 + i, :], I[name][l, :].rearrange("(a p) -> p a", p=128)).then_inc(vec_loaded, 16)
                pool.dma_start(flog[:, 0:4, :], I["cache_d_logf"][l, 0, :, :].rearrange("(t p) h -> p t h", p=128))\
                    .then_inc(fc_loaded, 16)

                def loads(j):
                    g, hh = GROUPS[j], j % 2
                    if j:
                        hold(prep_full, l * N_PREP + prep_no(j - 1, len(PREP[j - 1])))
                    if g == "A":
                        pool.dma_start(kcache[:, 3, 0:HD], I["cache_a_k"][l, 0, :, hh, :]).then_inc(kc_loaded, 16)
                    elif g in "BD":
                        src = (I["cache_b_k"][l, 0].rearrange("(t p) h c d -> p t (h c d)", p=128) if g == "B"
                               else I["cache_d_k"][l, 0].rearrange("(t p) h d -> p t (h d)", p=128))
                        pool.dma_start(kcache[:, :, :], src[:, :, hh * 256:(hh + 1) * 256]).then_inc(kc_loaded, 16)
                    elif hh == 0:
                        pool.dma_start(kcache[:, :, 0:CKVR], I["cache_c_kv"][l, 0].rearrange("(t p) d -> p t d", p=128))\
                            .then_inc(kc_loaded, 16)
                        pool.dma_start(kcache[:, :, CKVR:CKVR + ROPE],
                                       I["cache_c_krope"][l, 0].rearrange("(t p) d -> p t d", p=128)).then_inc(kc_loaded, 16)
                    hold(job_out, l * 8 + j + 1)
                    if g == "A":
                        pool.dma_start(vtok[:, 3, 0:HD], I["cache_a_v"][l, 0, :, hh, :]).then_inc(vc_loaded, 16)
                    elif g in "BD":
                        src = (I["cache_b_v"][l, 0].rearrange("(t p) h d -> p t (h d)", p=128) if g == "B"
                               else I["cache_d_v"][l, 0].rearrange("(t p) h d -> p t (h d)", p=128))
                        pool.dma_start(vtok[:, 0:4, :], src[:, :, hh * 256:(hh + 1) * 256]).then_inc(vc_loaded, 16)

                def store(dst, src):
                    pool.dma_start(dst, src).then_inc(stored, 16)

                def store_group(n, pairs):
                    hold(group_ready, l * 4 + n + 1)
                    for out_p, out_s, c, w in pairs:
                        store(out_p.rearrange("(t p) n -> p t n", p=128), proj("ABCD"[n])[:, 0:2, c:c + w])
                        store(out_s, proj("ABCD"[n])[0:DSEQ, 2, c:c + w])

                def stored_group(n):
                    pool.wait_ge(stored, 16 * (l * N_STORED + STORED[n]))
                    pool.sem_inc(proj_free, 1)

                loads(0)
                hold(group_ready, l * 4 + 1)
                for out_p, out_s, cache, c in (("a_k_p", "a_k_s", "cache_a_k", 512), ("a_v_p", "a_v_s", "cache_a_v", 640)):
                    store(O[out_p][l, 0].rearrange("t h d -> t (h d)"), proj("A")[:, 1, c:c + 128])
                    store(O[out_s][l, 0, DSEQ:WINDOW].rearrange("t h d -> t (h d)"), proj("A")[0:DSEQ, 2, c:c + 128])
                    store(O[out_s][l, 0, 0:DSEQ].rearrange("t h d -> t (h d)"),
                          I[cache][l, 0, DSEQ:WINDOW].rearrange("t h d -> t (h d)"))
                loads(1)
                stored_group(0)
                loads(2)
                store_group(1, [(O["b_k_p"][l, 0].rearrange("t h c d -> t (h c d)"),
                                 O["b_k_s"][l, 0].rearrange("t h c d -> t (h c d)"), 512, 512),
                                (O["b_v_p"][l, 0].rearrange("t h d -> t (h d)"),
                                 O["b_v_s"][l, 0].rearrange("t h d -> t (h d)"), 1024, 512)])
                loads(3)
                stored_group(1)
                loads(4)
                store_group(2, [(O["c_kv_p"][l, 0], O["c_kv_s"][l, 0], CQR, CKVR),
                                (O["c_krope_p"][l, 0], O["c_krope_s"][l, 0], 512, ROPE)])
                loads(5)
                stored_group(2)
                loads(6)
                store_group(3, [(O["d_k_p"][l, 0].rearrange("t h d -> t (h d)"),
                                 O["d_k_s"][l, 0].rearrange("t h d -> t (h d)"), 512, 512),
                                (O["d_v_p"][l, 0].rearrange("t h d -> t (h d)"),
                                 O["d_v_s"][l, 0].rearrange("t h d -> t (h d)"), 1024, 512)])
                store(O["d_logf_p"][l, 0].rearrange("(t p) h -> p t h", p=128), flog[:, 5:7, :])
                store(O["d_logf_s"][l, 0], flog[0:DSEQ, 4, :])
                loads(7)
                stored_group(3)
                def lower_half(u4, s):
                    hold(hi_ready, l * TAIL + RING * u4 + s + 1)
                    nc.gpsimd.tensor_tensor(wlo[:, s, :], ring[:, s, :], whi[:, s, :].bitcast(f32), ALU.subtract)\
                        .then_inc(lo_ready, 1)

                lower_half(0, 0)
                lower_half(0, 1)
                hold(job_out, l * 8 + 9)
                pool.dma_start(otmp[:, 0:2, :], I["p_prompt"][l, 0].rearrange("(t p) n -> p t n", p=128)).then_inc(ple_loaded, 16)
                pool.dma_start(otmp[0:DSEQ, 2, :], I["p_sample"][l, 0]).then_inc(ple_loaded, 16)
                lower_half(0, 2)
                lower_half(0, 3)
                with pool.Fori(1, TAIL // RING) as u4:
                    for s in range(RING):
                        lower_half(u4, s)
            hold(stored, 16 * N_STORED * DEPTH)

        N_VEC = len(VECS) + 2
        KC = [1, 2, 3, 4, 6, 6, 7, 8]
        VC = [1, 2, 3, 4, 4, 4, 5, 6]

        @block.tensor
        def _(pe):
            mm = nc.tensor.matmul

            def hold(s, value):
                pe.wait_ge(s, value)
                pe.sem_inc(pe_passed, 1)

            def unit(l, n):
                hold(raw_loaded[n % RING], 16 * (l * SLOT + n // RING + 1))
                return ring[:, n % RING, :]

            def tail_unit(l, q4, u):
                hold(lo_ready, l * TAIL + 4 * q4 + u + 1 - TAIL0)
                return [w[:, u % RING, :].rearrange("p (a n) -> p a n", a=UK) for w in (whi, wlo)]

            def product(out, w, k, m, x2, start, stop):
                (hi, lo), (xh, xl), cols = w, x2, slice(m * 128, (m + 1) * 128)
                mm(out, lo[:, k, cols], xh, start=start, stop=False)
                mm(out, hi[:, k, cols], xl, start=False, stop=False)
                return mm(out, hi[:, k, cols], xh, start=False, stop=stop)

            def gemm_chunk(l, q4, half, chunk_no, src, before_unit=None, before_last=None, units=KB // UK, first=0):
                nk = UK
                hold(half_free, l * CHUNKS + chunk_no + 1)
                for u in range(units):
                    w = tail_unit(l, q4, first + u)
                    if before_unit:
                        before_unit(u)
                    for m in range(4):
                        if m == 3 and u == 0 and before_last:
                            before_last()
                        for k in range(nk):
                            last = product(ps[:, 4 * half + m, 0:TOK], w, k, m, src(u * nk + k),
                                           u == 0 and k == 0, u == units - 1 and k == nk - 1)
                        if u == units - 1 and m < 3:
                            last.then_inc(bank_full, 1)
                    last.then_inc(unit_used, 1)

            def x_block(k):
                return xhi[:, k, :], xlo[:, k, :]

            def hid_block(k):
                return hhi[:, k, :], hlo[:, k, :]

            def transpose_embeddings(l):
                hold(ple_loaded, 32 * (l + 1))
                hold(half_free, l * CHUNKS + 4)
                for fb in range(2):
                    for t, o, n in ((0, 0, 128), (1, 128, 128), (2, 256, DSEQ)):
                        last = tr(ps[:, 4 + fb, o:o + n], otmp[0:n, t, fb * 128:(fb + 1) * 128])
                last.then_inc(pleT_full, 1)

            def rms_feature(l, p, half):
                hold(acc_ready, l * 3 + p + 1)
                mm(ps[:, 4 * half + 3, 0:TOK], ones[:, :], acc[:, 0:TOK], start=True, stop=True).then_inc(rms_summed, 1)

            def w_in_piece(l, no, u, t):
                _, units, nk, ncol, _ = CHUNK_AT[no]
                if (u, t) == (0, 0) and no == WIN["D"][0][0]:
                    hold(wout_added, l * 2 * KB + KB)
                elif (u, t) == (0, 0) and no > 1:
                    hold(proj_copied, l * N_WIN + (1 if no == 2 else no))
                if t == 0:
                    unit(l, POS[no, u])
                    if no == 0:
                        hold(gained, l * KB + min(KB, (u + 1) * nk + 1))
                w, out = ring[:, POS[no, u] % RING, :], ps[:, chunk_bank(no) + t, :]
                wv = w[:, 0:nk * ncol].rearrange("p (a n) -> p a n", a=nk)
                for k in range(nk):
                    kk = u * nk + k
                    last = mm(out[:, 0:ncol], xg[:, kk * TOK + t * 128:kk * TOK + t * 128 + 128], wv[:, k, :],
                              start=(kk == 0), stop=(kk == KB - 1))
                if t == 2:
                    last.then_inc(unit_used, 1)
                elif u == units - 1:
                    last.then_inc(proj_full, 1)

            def w_out_block(l, r, b, part):
                if part == 0 and b < 3:
                    hold(proj_copied, l * N_WIN + (7, 11)[r])
                elif part == 0:
                    hold(wout_added, l * 2 * KB + r * KB + b - 2)
                k0, k1 = OUT_K[r]
                per_unit = (2, 1)[r]
                at = POS[f"out{r}", b // per_unit]
                if b % per_unit == 0 and part == 0:
                    unit(l, at)
                w = ring[:, at % RING, :].rearrange("p (a n) -> p a n", a=k1 - k0)
                c = b % per_unit * 128
                for k in range(k0 + 4 * part, k0 + 4 * part + 4):
                    last = mm(ps[:, out_bank(b), 0:TOK], w[:, k - k0, c:c + 128], hid[:, k, :], start=(k == k0), stop=(k == k1 - 1))
                if part == OUT_PARTS[r] - 1:
                    last.then_inc(unit_used if b % per_unit == per_unit - 1 else wout_full, 1)

            def fill(l, j, place):
                for no, u, t in AT.get((j, place), []):
                    w_in_piece(l, no, u, t)
                for r, b, part in OUT_AT.get((j, place), []):
                    w_out_block(l, r, b, part)

            def tr(out, in_):
                return nc.tensor.transpose(out, in_, ident[0:in_.shape[0], 0:in_.shape[0]])

            def prep(l, j):
                g = GROUPS[j] if j != "lat" else None
                for i, (what, m) in enumerate(PREP[j]):
                    b = i % 4
                    if i >= 4:
                        a, d = prep_waits(l, j, i - 3)
                        hold(prep_copied[i % 2], (a, d)[i % 2])
                    if what in ("q", "cq", "kn", "ckvn"):
                        src = {"q": lambda t: query_src(j, m, t), "kn": lambda t: new_key_src(j, m, t),
                               "cq": lambda t: proj_ac[:, t, m * 128:(m + 1) * 128],
                               "ckvn": lambda t: proj_ac[:, t, CQR:CQR + CKVR]}[what]
                        w = src(0).shape[1]
                        o = DSEQ if what in ("kn", "ckvn") else 0
                        tr(ps[0:w, b, o:o + 128], src(0)[:, :])
                        tr(ps[0:w, b, o + 128:o + 256], src(1)[:, :])
                        s = 0 if o else 256
                        tr(ps[0:w, b, s:s + DSEQ], src(2)[0:DSEQ, :]).then_inc(prep_full, 1)
                    else:
                        for t in range(3 if g == "A" else 0, 4):
                            src = kcache[:, t, 0:CKVR] if what == "ckvc" else cached_key_src(j, m, t)
                            last = tr(ps[0:src.shape[1], b, t * 128:(t + 1) * 128], src)
                        last.then_inc(prep_full, 1)

            def latents(l, j):
                hh = j - 4
                hold(pad_cleared, l + 1)
                a, d = prep_waits(l, "lat", len(PREP["lat"]))
                hold(prep_copied[0], a)
                hold(prep_copied[1], d)
                if hh:
                    hold(hid_copied, l * 16 + 2 * j)
                w = [unit(l, POS["lat", 4 * hh + k])[:, 0:MAPS * CEXT] for k in range(3)]
                for t in range(3):
                    for k in range(3):
                        last = mm(ps[:, t, 0:MAPS * CEXT], cqT[:, k * TOK + t * 128:k * TOK + t * 128 + 128],
                                  w[k], start=(k == 0), stop=(k == 2))
                    if t < 2:
                        last.then_inc(lat_full, 1)
                    else:
                        last.then_inc(unit_used, 3)
                wk = unit(l, POS["lat", 4 * hh + 3])[:, 0:512]
                for i in range(7):
                    off = i * 128 if i < 5 else KEYS + (i - 5) * 128
                    if i in (2, 3, 4):
                        hold(lat_copied[1], l * 12 + 6 * hh + i - 1)
                    if i == 5:
                        hold(lat_copied[0], l * 8 + 4 * hh + 1)
                    if i == 6:
                        hold(lat_copied[1], l * 12 + 6 * hh + 4)
                    last = mm(ps[:, lat_bank(i), :], ckvT[:, off:off + 128], wk, start=True, stop=True)
                    if i < 6:
                        last.then_inc(lat_full, 1)
                last.then_inc(unit_used, 1)

            def score_map(l, q):
                j, m = q // MAPS, q % MAPS
                g = GROUPS[j]
                S, K, km = scores(q), KEXTENT[g], (0 if g == "A" else m)
                k0, ns = PAST - cached_keys(g), samples(g)
                if g == "B" and m == 2:
                    hold(probs_ready, l * N_MAPS + q - 1)
                kk = kT[0:K, km, :]
                n0 = min(ns, 512)
                qs = qT[0:K, m, 256:TOK]
                mm(S[0:DSEQ, 0:n0], qs, kk[:, k0:k0 + n0], start=True, stop=True)
                if ns > 512:
                    mm(S[0:DSEQ, 512:ns], qs, kk[:, k0 + 512:k0 + ns], start=True, stop=True)
                mm(S[:, 576:704], qT[0:K, m, 0:128], kk[:, KEYS:KEYS + 128], start=True, stop=True)
                mm(S[:, 704:960], qT[0:K, m, 128:256], kk[:, KEYS:KEYS + 256], start=True, stop=True)\
                    .then_inc(scores_ready, 1)

            def transpose_probs(l, it):
                j, maps, _, _ = ITEMS[it]
                g = GROUPS[j]
                q = j * MAPS + maps[0]
                if g == "B":
                    hold(mix_ready, l * 4 + (it - 8) + 1)
                else:
                    hold(probs_ready, l * N_MAPS + q + 1)
                if it:
                    hold(probT_copied[0], l * N_ITEMS + it)
                    hold(probT_copied[1], l * N_ITEMS + it)
                P = prob[:, q % 4, :]
                prompt, sample = transposed(it)
                tr(prompt[:, 0:128], P[:, 576:704])
                tr(prompt[:, 128:256], P[:, 704:832])
                tr(prompt[:, 256:384], P[:, 832:960])
                nb = cached_keys(g) // 128
                for i in range(nb):
                    tr(sample[:, i * 64:(i + 1) * 64], P[0:DSEQ, i * 128:(i + 1) * 128])
                tr(sample[0:DSEQ, nb * 64:(nb + 1) * 64], P[0:DSEQ, nb * 128:nb * 128 + 64]).then_inc(probsT_ready, 1)

            def weigh_values(l, it):
                j, maps, col, w = ITEMS[it]
                g = GROUPS[j]
                if it:
                    hold(out_copied, l * N_ITEMS + it)
                nb = cached_keys(g) // 128
                for i in range(nb):
                    mm(ps[0:DSEQ, 4, 0:w], probT[:, 384 + i * 64:384 + (i + 1) * 64], values(j, col, w, 4 - nb + i),
                       start=(i == 0), stop=False)
                mm(ps[0:DSEQ, 4, 0:w], probT[0:DSEQ, 384 + nb * 64:384 + (nb + 1) * 64],
                   values(j, col, w, 4)[0:DSEQ, :], start=False, stop=True)
                mm(ps[:, 4, w:2 * w], probT[:, 0:128], values(j, col, w, 5), start=True, stop=True)
                mm(ps[:, 4, 2 * w:3 * w], probT[:, 128:256], values(j, col, w, 5), start=True, stop=False)
                mm(ps[:, 4, 2 * w:3 * w], probT[:, 256:384], values(j, col, w, 6), start=False, stop=True)\
                    .then_inc(out_ready, 1)

            def attention(l, j):
                g = GROUPS[j]
                fill(l, j, "copied")
                hold(vc_loaded, 16 * (l * VC[-1] + VC[j]))
                its = [i for i, it in enumerate(ITEMS) if it[0] == j]
                a, d = prep_waits(l, j, len(PREP[j]))
                hold(prep_copied[0], a)
                hold(prep_copied[1], d)
                for m in ITEMS[its[0]][1]:
                    score_map(l, j * MAPS + m)
                for i, it in enumerate(its):
                    following = ITEMS[it + 1][1] if it + 1 in its else ()
                    fill(l, j, f"S{i}")
                    for m in following[0:1]:
                        score_map(l, j * MAPS + m)
                    fill(l, j, f"T{i}")
                    transpose_probs(l, it)
                    fill(l, j, f"V{i}")
                    hold(probT_copied[0], l * N_ITEMS + it + 1)
                    hold(probT_copied[1], l * N_ITEMS + it + 1)
                    for m in following[1:2]:
                        score_map(l, j * MAPS + m)
                    weigh_values(l, it)
                fill(l, j, "out")
                hold(job_out, l * 8 + j + 2)
                for fb in range(2):
                    b = 4 - fb
                    for t, o, n in ((0, 256, DSEQ), (1, 0, 128), (2, 128, 128)):
                        last = tr(ps[:, b, o:o + n], otok[0:n, t, fb * 128:(fb + 1) * 128])
                    last.then_inc(oT_full, 1)

            hold(table_loaded, 16)
            hold(cleared, 1)
            hold(x_loaded, 48)
            hold(x_copied, 1)
            hflat = hid[:, :, :].rearrange("p a b -> p (a b)")
            for k in range(KB):
                if k >= 8:
                    hold(x_copied, k - 8 + 2)
                tr(ps[:, k % 8, 0:128], hflat[:, k * 128:(k + 1) * 128])
                tr(ps[:, k % 8, 128:256], hflat[:, DM + k * 128:DM + (k + 1) * 128])
                tr(ps[:, k % 8, 256:TOK], arena[0:DSEQ, k * 128:(k + 1) * 128]).then_inc(x_full, 1)
            pe.sem_inc(unit_used, RING)
            with pe.Fori(0, DEPTH) as l:
                hold(half_free, l * CHUNKS + 2)
                for no, u, t in pieces("A"):
                    w_in_piece(l, no, u, t)
                    if (no, u, t) == (0, 7, 2):
                        hold(acc_ready, l * 3 + 1)
                        for tile in range(3):
                            last = mm(ps[:, 3, tile:tile + 1], acc[:, tile * 128:(tile + 1) * 128], ones[:, 0:1],
                                      start=True, stop=True)
                        last.then_inc(rms_summed, 1)
                for j, g in enumerate(GROUPS):
                    if j in (5, 6):
                        hold(hid_copied, l * 16 + 2 * j)
                    if j == 4:
                        fill(l, j, "norm")
                        hold(hid_copied, l * 16 + 2 * j)
                        hold(group_ready, l * 4 + 3)
                        hold(kc_loaded, 16 * (l * KC[-1] + KC[4]))
                        prep(l, "lat")
                    if g == "C":
                        latents(l, j)
                        fill(l, j, "lat")
                    if j == 6:
                        fill(l, j, "norm")
                        hold(flog_ready, l + 1)
                        hold(fc_loaded, 16 * (l + 1))
                        for tiles in ([0, 1, 2, 3, 4], [5, 6]):
                            for n, t in enumerate(tiles):
                                rows = DSEQ if t == 4 else 128
                                for e in tiles[:n]:
                                    mm(ps[:, 0, t * 8:(t + 1) * 8], ones[:, :], flog[:, e, :], start=(e == tiles[0]), stop=False)
                                last = mm(ps[:, 0, t * 8:(t + 1) * 8], tri[0:rows, :], flog[0:rows, t, :], start=(n == 0), stop=True)
                        last.then_inc(fcum_full, 1)
                    fill(l, j, "prep")
                    if j in (1, 2, 3, 7):
                        hold(hid_copied, l * 16 + 2 * j)
                    if g in "AB":
                        hold(kc_loaded, 16 * (l * KC[-1] + KC[j]))
                        hold(group_ready, l * 4 + "ABCD".index(g) + 1)
                    else:
                        hold(ext_ready, l * 4 + j - 3)
                    prep(l, j)
                    attention(l, j)
                for c in range(4):
                    if c == 1:
                        hold(wout_added, (l + 1) * 2 * KB)
                    gemm_chunk(l, TAIL0 // RING, c % 2, c, lambda k: hid_block(OUT_K[1][1] + k), units=2, first=2 * c,
                               before_unit=((lambda u: hold(split_ready, l * 36 + 2 * u + 2)) if c == 0 else
                                            (lambda u: transpose_embeddings(l) if u == 1 else None) if c == 2 else None),
                               before_last=(lambda: hold(hid_copied, (l + 1) * 16)) if c == 0 else None)
                    if c == 2:
                        hold(pleT_copied, l + 1)
                with pe.Fori(0, FG) as g:
                    for c in range(4):
                        gemm_chunk(l, Q_MLP + 16 * g + 2 * c, c % 2, 4 + 8 * g + c, x_block,
                                   before_unit=(lambda u: hold(split_ready, l * 36 + 4 + 2 * u + 2)) if c == 0 else None,
                                   before_last=(lambda: hold(rms_ready, l * N_RMS + g + 2)) if c == 1 else None)
                        if c == 0:
                            hold(half_free, l * CHUNKS + 8 * g + 6)
                            rms_feature(l, 1, 1)
                    for c in range(4):
                        gemm_chunk(l, Q_MLP + 8 + 16 * g + 2 * c, c % 2, 8 + 8 * g + c, hid_block,
                                   before_unit=(lambda u: hold(hid_ready, l * 64 + g * 16 + 2 * u + 2)) if c == 0 else None)
                for c in range(4):
                    hold(half_free, l * CHUNKS + 36 + c + 1)
                    w = tail_unit(l, Q_PLE, c)
                    for m in range(4):
                        for k in range(2):
                            last = product(ps[:, 4 * (c % 2) + m, 0:TOK], w, k, m, (pleh[:, k, :], plel[:, k, :]),
                                           k == 0, k == 1)
                        last.then_inc(bank_full if m < 3 else unit_used, 1)
                for c in range(4):
                    gemm_chunk(l, Q_PLE + 1 + 2 * c, c % 2, 40 + c, x_block,
                               before_unit=(lambda u: hold(split_ready, l * 36 + 20 + 2 * u + 2)) if c == 0 else None,
                               before_last=(lambda: hold(rms_ready, l * N_RMS + N_RMS)) if c == 1 else None)
                    if c == 0:
                        hold(half_free, l * CHUNKS + 42)
                        rms_feature(l, 2, 1)
            hold(half_free, DEPTH * CHUNKS + 2)
            for i in range(12):
                t, q = i // 4, i % 4
                if i >= 8:
                    hold(y_copied, i - 7)
                n = 128 if t < 2 else DSEQ
                for k in range(4):
                    last = tr(ps[0:n, i % 8, k * 128:(k + 1) * 128], x[:, q * 4 + k, t * 128:t * 128 + n])
                last.then_inc(y_full, 1)

        def norm_views(name):
            if name in "ABD":
                h = 10 if name == "A" else 16
                return [(proj(name)[:, :, 0:h * HD].rearrange("p t (h d) -> p t h d", d=HD), 3, h, HD, 0)]
            if name == "C":
                return [(proj_ac[:, :, a:a + w].rearrange("p t (h d) -> p t h d", d=w), 3, 1, w, 3 * i)
                        for i, (a, w) in enumerate(((0, CQR), (CQR, CKVR), (512, ROPE)))]
            if name[0] == "L":
                return [(kext[:, :, :, 0:HD], 7, MAPS, HD, 0), (qext[:, :, :, 0:HD], 3, MAPS, HD, 28),
                        (qext[:, :, :, HD:CEXT], 3, MAPS, ROPE, 40)]
            return [(otok[:, :, :].rearrange("p t (h d) -> p t h d", d=128), 3, 2, 128, 0)]

        def sq_views(name):
            out, at = [], 0
            for _, t, h, w, _ in norm_views(name):
                out.append(sq[:, at:at + t * h * w].rearrange("p (t h d) -> p t h d", t=t, h=h))
                at += t * h * w
            return out

        def prep_target(j, what, m, b):
            if what == "cq":
                return cqT[:, m * TOK:(m + 1) * TOK], ps[:, b, 0:TOK]
            if what == "ckvc":
                return ckvT[:, 0:PAST], ps[:, b, 0:PAST]
            if what == "ckvn":
                return ckvT[:, PAST:ALLK], ps[:, b, 0:TOK]
            K = KEXTENT[GROUPS[j]]
            if what == "q":
                return qT[0:K, m, :], ps[0:K, b, 0:TOK]
            if what == "kn":
                return kT[0:K, m, PAST:ALLK], ps[0:K, b, 0:TOK]
            k0 = PAST - cached_keys(GROUPS[j])
            return kT[0:K, m, k0:PAST], ps[0:K, b, k0:PAST]

        def scale_of(g):
            return CEXT ** -0.5 if g == "C" else HD ** -0.5

        @block.scalar
        def _(act):
            A = nc.scalar.activation

            def gain_pass(l):
                act.wait_ge(half_free, l * CHUNKS + 2)
                for b in range(KB):
                    A(xg[:, b * TOK:(b + 1) * TOK], x[:, b, :], ACT.Copy, scale=gains[:, 0, b:b + 1]).then_inc(gained, 1)

            def upper_halves(l, n, slots=range(RING)):
                for s in slots:
                    act.wait_ge(raw_loaded[s], 16 * (l * SLOT + n + 1))
                    act.wait_ge(unit_used, l * UNITS + RING * n + s + 1)
                    A(whi[:, s, :], ring[:, s, :], ACT.Copy).then_inc(hi_ready, 1)

            def sigmoids(l, c):
                for b in range(4 * c, 4 * c + 4):
                    act.wait_ge(sig_in, l * 16 + b + 1)
                    A(t1[:, b % 2, :], t0[:, b % 2, :], ACT.Sigmoid).then_inc(sig_ready, 1)

            def rms_root(l, n, src, dst):
                act.wait_ge(rms_summed, l * N_RMS + n + 1)
                A(dst, src, ACT.Sqrt, bias=eps[:, 0:1], scale=1.0 / DM).then_inc(rms_ready, 1)

            def norm(l, name):
                n = l * N_NORM + NORM[name] + 1
                for (src, t, h, w, _), dst in zip(norm_views(name), sq_views(name)):
                    last = A(dst, src, ACT.Square)
                last.then_inc(sq_ready, 1)
                act.wait_ge(ssq_ready, n)
                spans = {}
                for _, t, h, w, o in norm_views(name):
                    lo, hi = spans.get(w, (o, o))
                    spans[w] = (min(lo, o), max(hi, o + t * h))
                for w, (lo, hi) in spans.items():
                    last = A(root[:, lo:hi], ssq[:, lo:hi], ACT.Sqrt, bias=eps[:, 0:1], scale=1.0 / w)
                last.then_inc(root_ready, 1)

            def prep(l, j):
                for i in range(0, len(PREP[j]), 2):
                    what, m = PREP[j][i]
                    act.wait_ge(prep_full, l * N_PREP + prep_no(j, i) + 1)
                    dst, src = prep_target(j, what, m, i % 4)
                    A(dst, src, ACT.Copy).then_inc(prep_copied[0], 1)

            def exps(l, j, it, maps):
                g = GROUPS[j]
                for m in maps:
                    q = j * MAPS + m
                    S, P, ns = scores(q), prob[:, q % 4, :], samples(g)
                    act.wait_ge(shift_ready, l * N_MAPS + q + 1)
                    if it >= 2:
                        act.wait_ge(probsT_ready, l * N_ITEMS + it - 1)
                    if g == "A":
                        act.wait_ge(sink_ready, l * 8 + q + 1)
                        A(es[:, q, :], es[:, q, :], ACT.Exp, scale=scale_of(g))
                    for t, (lo, hi, n) in enumerate(((0, ns, DSEQ), (576, 704, 128), (704, 960, 128))):
                        last = A(P[0:n, lo:hi], S[0:n, lo:hi], ACT.Exp, bias=sm[0:n, q, t:t + 1], scale=scale_of(g),
                                 accum_out=sums[0:n, q, t:t + 1])
                    last.then_inc(probs_ready, 1)

            def attention(l, j):
                its = [i for i, it in enumerate(ITEMS) if it[0] == j]
                exps(l, j, its[0], ITEMS[its[0]][1])
                nb = cached_keys(GROUPS[j]) // 128
                for it in its:
                    following = ITEMS[it + 1][1] if it + 1 in its else ()
                    exps(l, j, it + 1, following[0:1])
                    act.wait_ge(probsT_ready, l * N_ITEMS + it + 1)
                    if it:
                        act.wait_ge(out_ready, l * N_ITEMS + it)
                    _, sample = transposed(it)
                    A(probT[:, 384:384 + nb * 64], sample[:, 0:nb * 64], ACT.Copy)
                    A(probT[0:DSEQ, 384 + nb * 64:448 + nb * 64], sample[0:DSEQ, nb * 64:nb * 64 + 64], ACT.Copy)\
                        .then_inc(probT_copied[0], 1)
                    exps(l, j, it + 1, following[1:2])
                if GROUPS[j] == "B":
                    act.wait_ge(out_copied, l * N_ITEMS + its[-1] + 1)
                    norm(l, f"O{j}")
                if j == len(GROUPS) - 1:
                    upper_halves(l, TAIL0 // RING, (0, 1))
                for fb in range(2):
                    act.wait_ge(oT_full, l * 16 + 2 * j + fb + 1)
                    A(hid[:, 2 * j + fb, :], ps[:, 4 - fb, 0:TOK], ACT.Copy).then_inc(hid_copied, 1)

            act.wait_ge(cleared, 1)
            with act.Fori(0, DEPTH) as l:
                act.wait_ge(mix_loaded, 16 * (l + 1))
                gain_pass(l)
                rms_root(l, 0, ps[:, 3, 0:3], rroot[:, 0:3])
                act.wait_ge(proj_copied, l * N_WIN + 2)
                norm(l, "A")
                for j, g in enumerate(GROUPS):
                    if j == 2:
                        act.wait_ge(lam_in, l + 1)
                        A(lam[:, 2:4], lam[:, 0:2], ACT.Exp).then_inc(lam_exp, 1)
                        act.wait_ge(proj_copied, l * N_WIN + 5)
                        norm(l, "B")
                    if j == 4:
                        act.wait_ge(proj_copied, l * N_WIN + 7)
                        norm(l, "C")
                        prep(l, "lat")
                    if g == "C":
                        hh = j - 4
                        for i in range(0, 7, 2):
                            if i < 6:
                                act.wait_ge(lat_full, l * 16 + 8 * hh + 2 + i + 1)
                            else:
                                act.wait_ge(unit_used, l * UNITS + POS["lat", 4 * hh + 3] + 1 + RING)
                            src = ps[:, lat_bank(i), :].rearrange("p (m d) -> p m d", m=MAPS)
                            A(kext[:, i, :, 0:HD], src[:, :, 0:HD], ACT.Copy)
                            A(vtok[:, i, :].rearrange("p (m d) -> p m d", m=MAPS), src[:, :, HD:128], ACT.Copy)\
                                .then_inc(lat_copied[0], 1)
                        act.wait_ge(lat_copied[1], l * 12 + 6 * hh + 6)
                        act.wait_ge(lat_copied[0], l * 8 + 4 * hh + 4)
                        norm(l, f"L{j}")
                    if j == 6:
                        act.wait_ge(proj_copied, l * N_WIN + 11)
                        act.wait_ge(fz_ready, 2 * l + 1)
                        A(fsm[:, 2, :], fsm[:, 1, :], ACT.Exp, scale=-1.0).then_inc(fz_act, 1)
                        norm(l, "D")
                        act.wait_ge(fz_ready, 2 * l + 2)
                        A(fsm[:, 5, :], fsm[:, 3, :], ACT.Ln).then_inc(fz_act, 1)
                    prep(l, j)
                    attention(l, j)
                upper_halves(l, TAIL0 // RING, (2, 3))
                upper_halves(l, TAIL0 // RING + 1)
                with act.Fori(0, FG) as g:
                    with act.Fori(0, 3) as i:
                        upper_halves(l, Q_MLP + 16 * g + i)
                    rms_root(l, 1 + g, ps[:, 7, 0:TOK], rroot[:, :])
                    with act.Fori(3, 16) as i:
                        upper_halves(l, Q_MLP + 16 * g + i)
                for i in range(9):
                    upper_halves(l, Q_PLE + i)
                    if i and i % 2 == 1 and i > 2:
                        c = (i - 3) // 2
                        if c == 0:
                            rms_root(l, 1 + FG, ps[:, 7, 0:TOK], rroot[:, :])
                        sigmoids(l, c)
                sigmoids(l, 3)

        @block.vector
        def _(dve):
            V = nc.vector
            STEPS = 1024
            count = [0]

            def done(ins):
                count[0] += 1
                ins.then_inc(step, 1)
                dve.wait_ge(step, here[0] + count[0])

            here = [None]

            def mul(out, a, b):
                return V.tensor_tensor(out, a, b, ALU.mult)

            def add(out, a, b):
                return V.tensor_tensor(out, a, b, ALU.add)

            def squares_pass(l, chunks):
                dve.wait_ge(half_free, l * CHUNKS + 2 + chunks)
                done(mul(hid[:, :, :], x[:, :, :], x[:, :, :]))
                V.tensor_reduce(acc[:, 0:TOK], hid[:, :, :].rearrange("p b t -> p t b"), X, ALU.add).then_inc(acc_ready, 1)

            def split_blocks(p, b0, b1):
                for b in range(b0, b1, 2):
                    for i in range(2):
                        last = V.tensor_scalar(xhi[:, b + i, :], x[:, b + i, :], gains[:, p, b + i:b + i + 1], None, ALU.mult)
                    done(last)
                    for i in range(2):
                        V.scalar_tensor_tensor(out=xlo[:, b + i, :], in0=x[:, b + i, :], scalar=gains[:, p, b + i:b + i + 1],
                                               in1=xhi[:, b + i, :].bitcast(f32), op0=ALU.mult, op1=ALU.subtract)\
                            .then_inc(split_ready, 1)

            def copy_chunk(l, no):
                _, units, nk, ncol, c0 = CHUNK_AT[no]
                g = [g for g in "ABCD" if CHUNK_AT[no] in WIN[g]][0]
                if no == WIN[g][0][0]:
                    dve.wait_ge(proj_free, l * 4 + {"A": 1, "B": 1, "C": 2, "D": 3}[g])
                for t in range(3):
                    if t < 2:
                        dve.wait_ge(proj_full, l * 2 * N_WIN + 2 * no + t + 1)
                    else:
                        dve.wait_ge(unit_used, l * UNITS + POS[no, units - 1] + 1 + RING)
                    if no == 0 and t == 0:
                        dve.wait_ge(rms_ready, l * N_RMS + 1)
                        done(V.reciprocal(rtok[:, :], rroot[:, 0:3]))
                    last = V.tensor_scalar(proj(g)[:, t, c0:c0 + ncol], ps[:, chunk_bank(no) + t, 0:ncol],
                                           rtok[:, t:t + 1], None, ALU.mult)
                last.then_inc(proj_copied, 1)

            def filled(l, j, place):
                for no, u, t in AT.get((j, place), []):
                    if t == 2 and u == CHUNK_AT[no][1] - 1:
                        copy_chunk(l, no)
                for r, b, part in OUT_AT.get((j, place), []):
                    if part < OUT_PARTS[r] - 1:
                        continue
                    if r == 0 and b % 2 == 0:
                        dve.wait_ge(wout_full, l * KB // 2 + b // 2 + 1)
                    else:
                        dve.wait_ge(unit_used, l * UNITS + POS[f"out{r}", b // (2, 1)[r]] + 1 + RING)
                    add(x[:, b, :], ps[:, out_bank(b), 0:TOK], x[:, b, :]).then_inc(wout_added, 1)

            def norm(l, name):
                n = l * N_NORM + NORM[name] + 1
                dve.wait_ge(sq_ready, n)
                for (_, t, h, w, o), s in zip(norm_views(name), sq_views(name)):
                    last = V.tensor_reduce(ssq[:, o:o + t * h], s, X, ALU.add)
                last.then_inc(ssq_ready, 1)
                tot = sum(t * h for _, t, h, _, _ in norm_views(name))
                dve.wait_ge(root_ready, n)
                done(V.reciprocal(rstd[:, 0:tot], root[:, 0:tot]))
                for view, t, h, w, o in norm_views(name):
                    r = rstd[:, o:o + t * h].rearrange("p (t h) -> p t h", t=t).unsqueeze(3).broadcast_to([128, t, h, w])
                    last = mul(view, view, r)
                done(last)

            def gain(view, g, t, h, w):
                return mul(view, view, g.unsqueeze(1).unsqueeze(1).broadcast_to([128, t, h, w]))

            def heads(g, a, b, d=HD):
                return proj(g)[:, :, a:b].rearrange("p t (h d) -> p t h d", d=d)

            def rope(x1, x2, c, s, a, b):
                mul(a, x2, s)
                done(mul(b, x1, s))
                mul(x1, x1, c)
                done(mul(x2, x2, c))
                V.tensor_tensor(x1, x1, a, ALU.subtract)
                return add(x2, x2, b)

            def prep(l, j):
                for i in range(1, len(PREP[j]), 2):
                    what, m = PREP[j][i]
                    dve.wait_ge(prep_full, l * N_PREP + prep_no(j, i) + 1)
                    dst, src = prep_target(j, what, m, i % 4)
                    V.tensor_copy(dst, src).then_inc(prep_copied[1], 1)

            def bias_and_max(l, j, maps):
                g, hh = GROUPS[j], j % 2
                for m in maps:
                    q = j * MAPS + m
                    S, ns = scores(q), samples(g)
                    dve.wait_ge(scores_ready, l * N_MAPS + q + 1)
                    if g in "AB":
                        slope = (SLOPE_A[hh * 4 + m] if g == "A" else SLOPE_B[hh * 2 + m // 2]) / scale_of(g)
                        nd = T_NDA if g == "A" else T_NDB
                        for n, lo, hi, c in ((DSEQ, 0, ns, T_NDS + 576 - ns), (128, 576, 704, nd + 128), (128, 704, 960, nd)):
                            last = V.scalar_tensor_tensor(out=S[0:n, lo:hi], in0=table[0:n, c:c + hi - lo], scalar=slope,
                                                          in1=S[0:n, lo:hi], op0=ALU.mult, op1=ALU.add)
                        done(last)
                    else:
                        mask = table[:, T_MC:T_MC + 128] if g == "C" else table[:, T_MD:T_MD + 128]
                        if g == "D":
                            add(S[0:DSEQ, 512:576], S[0:DSEQ, 512:576], mask[0:DSEQ, 0:DSEQ])
                        add(S[:, 576:704], S[:, 576:704], mask)
                        done(add(S[:, 832:960], S[:, 832:960], mask))
                    for t, (lo, hi, n) in enumerate(((0, ns, DSEQ), (576, 704, 128), (704, 960, 128))):
                        last = V.tensor_reduce(mx[0:n, q, t:t + 1], S[0:n, lo:hi], X, ALU.max)
                    done(last)
                    if g == "A":
                        sink = v("a_sinks")[:, q:q + 1].broadcast_to([128, 3])
                        done(V.tensor_tensor(mx[:, q, :], mx[:, q, :], sink, ALU.max))
                        V.tensor_tensor(es[:, q, :], sink, mx[:, q, :], ALU.subtract).then_inc(sink_ready, 1)
                    V.tensor_scalar(sm[:, q, :], mx[:, q, :], -scale_of(g), None, ALU.mult).then_inc(shift_ready, 1)

            def attention(l, j):
                g, hh = GROUPS[j], j % 2
                its = [i for i, it in enumerate(ITEMS) if it[0] == j]
                filled(l, j, "copied")
                bias_and_max(l, j, ITEMS[its[0]][1])
                for i, it in enumerate(its):
                    _, maps, col, w = ITEMS[it]
                    q = j * MAPS + maps[0]
                    following = ITEMS[it + 1][1] if it + 1 in its else ()
                    filled(l, j, f"S{i}")
                    bias_and_max(l, j, following[0:1])
                    dve.wait_ge(probs_ready, l * N_MAPS + j * MAPS + maps[-1] + 1)
                    if g == "A":
                        done(add(sums[:, q, :], sums[:, q, :], es[:, q, :]))
                    done(V.reciprocal(rinv[:, q:q + len(maps), :], sums[:, q:q + len(maps), :]))
                    if g == "B":
                        done(V.tensor_scalar(rinv[:, q + 1, :], rinv[:, q + 1, :], lam[:, 5:6], None, ALU.mult))
                        P0, P1 = prob[:, q % 4, :], prob[:, q % 4 + 1, :]
                        spans = ((0, 576, DSEQ), (576, 704, 128), (704, 960, 128))
                        for t, (lo, hi, n) in enumerate(spans):
                            last = V.tensor_scalar(P1[0:n, lo:hi], P1[0:n, lo:hi], rinv[0:n, q + 1, t:t + 1], None, ALU.mult)
                        done(last)
                        for t, (lo, hi, n) in enumerate(spans):
                            last = V.scalar_tensor_tensor(out=P0[0:n, lo:hi], in0=P0[0:n, lo:hi], scalar=rinv[0:n, q, t:t + 1],
                                                          in1=P1[0:n, lo:hi], op0=ALU.mult, op1=ALU.subtract)
                        last.then_inc(mix_ready, 1)
                    dve.wait_ge(probsT_ready, l * N_ITEMS + it + 1)
                    if it:
                        dve.wait_ge(out_ready, l * N_ITEMS + it)
                    V.tensor_copy(probT[:, 0:384], transposed(it)[0][:, 0:384]).then_inc(probT_copied[1], 1)
                    filled(l, j, f"T{i}")
                    bias_and_max(l, j, following[1:2])
                    dve.wait_ge(out_ready, l * N_ITEMS + it + 1)
                    if it == its[0] and j:
                        dve.wait_ge(oT_full, l * 16 + 2 * j)
                    o = ps[:, 4, 0:3 * w].rearrange("p (t d) -> p t d", t=3)
                    if g == "B":
                        last = V.tensor_copy(otok[:, :, col:col + w], o)
                    else:
                        last = mul(otok[:, :, col:col + w], o, rinv[:, q, :].unsqueeze(2).broadcast_to([128, 3, w]))
                    if g == "B" or it != its[-1]:
                        last.then_inc(out_copied, 1)
                    else:
                        done(last)
                        V.tensor_copy(otmp[:, 0, 0:1], otok[:, 0, 0:1]).then_inc(out_copied, 1)
                    filled(l, j, f"V{i}")
                if g == "B":
                    norm(l, f"O{j}")
                    gain(otok[:, :, :].rearrange("p t (h d) -> p t h d", d=128), v("b_gout"), 3, 2, 128).then_inc(job_out, 1)
                else:
                    V.tensor_copy(otmp[:, 0, 1:2], otok[:, 0, 0:1]).then_inc(job_out, 1)
                filled(l, j, "out")

            def block_done(l, n0, no, m, units=8):
                if m < 3:
                    dve.wait_ge(bank_full, l * 3 * CHUNKS + 3 * no + m + 1)
                else:
                    dve.wait_ge(unit_used, l * UNITS + n0 + units + RING)

            def add_chunk(l, n0, no, half, blk, units=8):
                for m in range(4):
                    block_done(l, n0, no, m, units)
                    d = x[:, blk + m, :] if isinstance(blk, int) else x[:, bass.ds(blk + m, 1), :]
                    s = ps[:, 4 * half + m, 0:TOK] if isinstance(blk, int) else ps[:, 4 * half + m:4 * half + m + 1, 0:TOK]
                    last = add(d, s, d)
                last.then_inc(half_free, 1)

            V.memset(ps[:, :, :], 0.0).then_inc(x_copied, 1)
            dve.sem_inc(job_out, 1)
            dve.wait_ge(cleared, 1)
            for k in range(KB):
                dve.wait_ge(x_full, k + 1)
                last = V.tensor_copy(x[:, k, :], ps[:, k % 8, 0:TOK])
                if k < KB - 1:
                    last.then_inc(x_copied, 1)
            last.then_inc(half_free, 2)
            dve.wait_ge(half_free, 2)
            with dve.Fori(0, DEPTH) as l:
                here[0] = l * STEPS
                count[0] = 0
                squares_pass(l, 0)
                copy_chunk(l, 0)
                copy_chunk(l, 1)
                dve.wait_ge(vec_loaded, 16 * N_VEC * (l + 1))
                V.tensor_scalar(v("a_sinks"), v("a_sinks"), HD ** 0.5, None, ALU.mult)
                V.tensor_scalar(v("b_gout"), v("b_gout"), vec[:, VOFF["lam_init"] + 1:VOFF["lam_init"] + 2], None, ALU.mult)
                mul(otmp[:, 0, 0:HD], v("b_lq1"), v("b_lk1"))
                done(mul(otmp[:, 0, HD:2 * HD], v("b_lq2"), v("b_lk2")))
                V.tensor_reduce(lam[:, 0:2], otmp[:, 0, 0:2 * HD].rearrange("p (a d) -> p a d", a=2), X, ALU.add)\
                    .then_inc(lam_in, 1)
                norm(l, "A")
                gain(heads("A", 0, 512), v("a_gq"), 3, 8, HD)
                gain(heads("A", 512, 640), v("a_gk"), 3, 2, HD).then_inc(group_ready, 1)
                for j, g in enumerate(GROUPS):
                    if j == 2:
                        dve.wait_ge(lam_exp, l + 1)
                        done(V.tensor_tensor(lam[:, 4:5], lam[:, 2:3], lam[:, 3:4], ALU.subtract))
                        done(add(lam[:, 5:6], lam[:, 4:5], vec[:, VOFF["lam_init"]:VOFF["lam_init"] + 1]))
                        norm(l, "B")
                        gain(heads("B", 0, 512), v("b_gq"), 3, 8, HD)
                        gain(heads("B", 512, 1024), v("b_gk"), 3, 8, HD).then_inc(group_ready, 1)
                    if j == 4:
                        norm(l, "C")
                        mul(proj_ac[:, :, 0:512], proj_ac[:, :, 0:512],
                            vec[:, VOFF["c_gcq"]:VOFF["c_gcq"] + 512].unsqueeze(1).broadcast_to([128, 3, 512]))
                        done(mul(proj_ac[:, :, 512:544], proj_ac[:, :, 512:544],
                                 v("c_gkr").unsqueeze(1).broadcast_to([128, 3, ROPE])))
                        a = otmp[:, 0, 0:48].rearrange("p (t n) -> p t n", t=3)
                        b = otmp[:, 0, 48:96].rearrange("p (t n) -> p t n", t=3)
                        rope(proj_ac[:, :, 512:528], proj_ac[:, :, 528:544], cos, sin, a, b).then_inc(group_ready, 1)
                        prep(l, "lat")
                        filled(l, j, "norm")
                    if g == "C":
                        hh = j - 4
                        for t in range(3):
                            if t < 2:
                                dve.wait_ge(lat_full, l * 16 + 8 * hh + t + 1)
                            else:
                                dve.wait_ge(unit_used, l * UNITS + POS["lat", 4 * hh + 2] + 1 + RING)
                            V.tensor_copy(qext[:, t, :, :], ps[:, t, 0:MAPS * CEXT].rearrange("p (m d) -> p m d", m=MAPS))\
                                .then_inc(lat_copied[1], 1)
                        for i in (1, 3, 5):
                            dve.wait_ge(lat_full, l * 16 + 8 * hh + 2 + i + 1)
                            src = ps[:, lat_bank(i), :].rearrange("p (m d) -> p m d", m=MAPS)
                            V.tensor_copy(kext[:, i, :, 0:HD], src[:, :, 0:HD])
                            V.tensor_copy(vtok[:, i, :].rearrange("p (m d) -> p m d", m=MAPS), src[:, :, HD:128])\
                                .then_inc(lat_copied[1], 1)
                        norm(l, f"L{j}")
                        gain(kext[:, :, :, 0:HD], v("c_gkn"), 7, MAPS, HD)
                        done(gain(qext[:, :, :, :], vec[:, VOFF["c_gqn"]:VOFF["c_gqn"] + CEXT], 3, MAPS, CEXT))
                        a = otmp[:, 0, 0:192].rearrange("p (t m n) -> p t m n", t=3, m=MAPS)
                        b = otmp[:, 1, 0:192].rearrange("p (t m n) -> p t m n", t=3, m=MAPS)
                        c4 = cos.unsqueeze(2).broadcast_to([128, 3, MAPS, 16])
                        s4 = sin.unsqueeze(2).broadcast_to([128, 3, MAPS, 16])
                        rope(qext[:, :, :, HD:HD + 16], qext[:, :, :, HD + 16:CEXT], c4, s4, a, b)
                        dve.wait_ge(kc_loaded, 16 * (l * KC[-1] + KC[4]))
                        V.tensor_copy(kext[:, 0:4, :, HD:CEXT],
                                      kcache[:, 0:4, CKVR:CKVR + ROPE].unsqueeze(2).broadcast_to([128, 4, MAPS, ROPE]))
                        V.tensor_copy(kext[:, 4:5, :, HD:CEXT],
                                      proj_ac[:, 2:3, 512:544].unsqueeze(2).broadcast_to([128, 1, MAPS, ROPE]))
                        V.tensor_copy(kext[:, 5:7, :, HD:CEXT],
                                      proj_ac[:, 0:2, 512:544].unsqueeze(2).broadcast_to([128, 2, MAPS, ROPE]))\
                            .then_inc(ext_ready, 1)
                        filled(l, j, "lat")
                    if j == 6:
                        z, az, e, u, d, ln, r = (fsm[:, i, :] for i in range(7))
                        dve.wait_ge(proj_copied, l * N_WIN + 11)
                        done(add(z.rearrange("p (t h) -> p t h", t=3), proj_bd[:, :, 1536:1544],
                                 v("d_bf").unsqueeze(1).broadcast_to([128, 3, 8])))
                        done(V.tensor_scalar(az, z, -1.0, None, ALU.mult))
                        V.tensor_tensor(az, az, z, ALU.max).then_inc(fz_ready, 1)
                        norm(l, "D")
                        dve.wait_ge(fz_act, 2 * l + 1)
                        done(V.tensor_scalar(u, e, 1.0, None, ALU.add))
                        V.tensor_scalar(d, u, 1.0, 1e-30, ALU.subtract, ALU.add).then_inc(fz_ready, 1)
                        gain(heads("D", 0, 512), v("d_gq"), 3, 8, HD)
                        dve.wait_ge(fz_act, 2 * l + 2)
                        done(V.reciprocal(r, d))
                        done(V.tensor_scalar(ln, ln, 1e-30, None, ALU.add))
                        done(mul(r, r, ln))
                        done(mul(r, r, e))
                        dve.wait_ge(proj_free, l * 4 + 1)
                        zt, rt = z.rearrange("p (t h) -> p t h", t=3), r.rearrange("p (t h) -> p t h", t=3)
                        for o, i, n in ((5, 0, 2), (4, 2, 1)):
                            last = V.scalar_tensor_tensor(out=flog[:, o:o + n, :], in0=zt[:, i:i + n, :], scalar=0.0,
                                                          in1=rt[:, i:i + n, :], op0=ALU.min, op1=ALU.subtract)
                        last.then_inc(flog_ready, 1)
                        gain(heads("D", 512, 1024), v("d_gk"), 3, 8, HD).then_inc(group_ready, 1)
                        filled(l, j, "norm")
                        dve.wait_ge(group_ready, 4 * l + 4)
                        dve.wait_ge(fcum_full, l + 1)
                        done(V.tensor_copy(fcum[:, :, :], ps[:, 0, 0:56].rearrange("p (t h) -> p t h", t=7)))
                    if g == "D":
                        hh = j % 2
                        K, Q = kext_of("D"), qext_of("D")
                        dve.wait_ge(kc_loaded, 16 * (l * KC[-1] + KC[j]))
                        if hh:
                            dve.wait_ge(job_out, l * 8 + j + 1)
                        sel = slice(hh * 4, hh * 4 + 4)
                        V.tensor_copy(K[:, 0:4, :, 0:HD], kcache[:, :, :].rearrange("p t (m d) -> p t m d", m=MAPS))
                        nk = proj_bd[:, :, 512 + hh * 256:768 + hh * 256].rearrange("p t (m d) -> p t m d", m=MAPS)
                        nq = proj_bd[:, :, hh * 256:(hh + 1) * 256].rearrange("p t (m d) -> p t m d", m=MAPS)
                        V.tensor_copy(K[:, 4:5, :, 0:HD], nk[:, 2:3, :, :])
                        V.tensor_copy(K[:, 5:7, :, 0:HD], nk[:, 0:2, :, :])
                        V.tensor_copy(Q[:, :, :, 0:HD], nq)
                        V.tensor_scalar(K[:, :, :, HD], fcum[:, :, sel], -(HD ** 0.5), None, ALU.mult)
                        V.memset(K[:, :, :, HD + 1], 1.0)
                        V.memset(Q[:, :, :, HD], 1.0)
                        V.tensor_scalar(Q[:, 0:2, :, HD + 1], fcum[:, 5:7, sel], HD ** 0.5, None, ALU.mult)
                        V.tensor_scalar(Q[:, 2:3, :, HD + 1], fcum[:, 4:5, sel], HD ** 0.5, None, ALU.mult)\
                            .then_inc(ext_ready, 1)
                    prep(l, j)
                    filled(l, j, "prep")
                    attention(l, j)
                assert count[0] < STEPS - 40
                for i in range(2):
                    dve.wait_ge(hid_copied, l * 16 + 14 + 2 * i)
                    own, tmp = slice(OUT_K[1][1] + 2 * i, OUT_K[1][1] + 2 * i + 2), htmp[:, 2 * i:2 * i + 2, :]
                    done(V.tensor_copy(tmp, hid[:, own, :]))
                    done(V.tensor_tensor(hlo[:, own, :], hid[:, own, :], tmp.bitcast(f32), ALU.subtract))
                    V.tensor_copy(hhi[:, own, :], tmp.bitcast(f32)).then_inc(split_ready, 2)
                for c in range(4):
                    if c == 2:
                        dve.wait_ge(pleT_full, l + 1)
                        done(V.tensor_copy(pleh[:, :, :], ps[:, 4:6, 0:TOK]))
                        V.tensor_tensor(plel[:, :, :], ps[:, 4:6, 0:TOK], pleh[:, :, :].bitcast(f32), ALU.subtract)\
                            .then_inc(pleT_copied, 1)
                    add_chunk(l, TAIL0 + 2 * c, c, c % 2, 4 * c, units=2)
                    dve.wait_ge(half_free, l * CHUNKS + 2 + c + 1)
                    split_blocks(1, 4 * c, 4 * c + 4)
                squares_pass(l, 4)
                UP_STEPS = 2 * KB - 4
                with dve.Fori(0, FG) as g:
                    here[0] = l * STEPS + g * UP_STEPS
                    at0 = count[0]
                    dve.wait_ge(rms_ready, l * N_RMS + g + 2)
                    V.reciprocal(rfeat[:, :], rroot[:, :]).then_inc(inv_ready, 1)
                    dve.wait_ge(inv_ready, l * (FG + 1) + g + 1)
                    for c in range(4):
                        for m in range(4):
                            block_done(l, MLP0 + 64 * g + 8 * c, 4 + 8 * g + c, m)
                            ins = V.scalar_tensor_tensor(out=t0[:, m % 2, :], in0=ps[:, 4 * (c % 2) + m, 0:TOK], scalar=0.0,
                                                         in1=rfeat[:, :], op0=ALU.max, op1=ALU.mult)
                            if m < 3:
                                done(ins)
                            else:
                                ins.then_inc(half_free, 1)
                                dve.wait_ge(half_free, l * CHUNKS + 2 + 4 + 8 * g + c + 1)
                            mul(hhi[:, 4 * c + m, :], t0[:, m % 2, :], t0[:, m % 2, :])
                            done(mul(t1[:, m % 2, :], t0[:, m % 2, :], t0[:, m % 2, :]))
                            V.tensor_tensor(hlo[:, 4 * c + m, :], t1[:, m % 2, :], hhi[:, 4 * c + m, :].bitcast(f32),
                                            ALU.subtract).then_inc(hid_ready, 1)
                    assert count[0] - at0 == UP_STEPS
                    for c in range(4):
                        add_chunk(l, MLP0 + 32 + 64 * g + 8 * c, 8 + 8 * g + c, c % 2, 4 * c)
                here[0] = l * STEPS
                count[0] += (FG - 1) * UP_STEPS
                gain_blocks = 0
                for c in range(4):
                    for m in range(4):
                        block_done(l, MLP0 + 256 + c, 36 + c, m, 1)
                        last = V.tensor_copy(plout[:, 4 * c + m, :], ps[:, 4 * (c % 2) + m, 0:TOK])
                    last.then_inc(half_free, 1)
                    if c == 0:
                        dve.wait_ge(half_free, l * CHUNKS + 2 + 4 + 8 * FG)
                    if c:
                        n = 2 if c < 3 else KB - 4
                        split_blocks(2, gain_blocks, gain_blocks + n)
                        gain_blocks += n
                squares_pass(l, 4 + 8 * FG)
                dve.wait_ge(rms_ready, l * N_RMS + N_RMS)
                V.reciprocal(rfeat[:, :], rroot[:, :]).then_inc(inv_ready, 1)
                dve.wait_ge(inv_ready, (l + 1) * (FG + 1))

                def finish(b):
                    dve.wait_ge(sig_ready, l * 16 + b + 1)
                    done(mul(plout[:, b, :], t1[:, b % 2, :], plout[:, b, :]))
                    last = add(x[:, b, :], x[:, b, :], plout[:, b, :])
                    if b % 4 == 3:
                        last.then_inc(half_free, 1)

                for b in range(KB):
                    c, m = b // 4, b % 4
                    if b and m == 0:
                        finish(b - 1)
                    block_done(l, MLP0 + 260 + 8 * c, 40 + c, m)
                    mul(t0[:, b % 2, :], ps[:, 4 * (c % 2) + m, 0:TOK], rfeat[:, :]).then_inc(sig_in, 1)
                    if m:
                        finish(b - 1)
                finish(KB - 1)
                V.memset(lam[:, 7:8], 0.0).then_inc(step, STEPS - count[0])
                dve.wait_ge(half_free, (l + 1) * CHUNKS + 2)
            hflat = hid[:, :, :].rearrange("p a b -> p (a b)")
            for i in range(12):
                t, q = i // 4, i % 4
                n = 128 if t < 2 else DSEQ
                dve.wait_ge(y_full, i + 1)
                dst = hflat[:, t * DM + q * 512:t * DM + (q + 1) * 512] if t < 2 else arena[0:DSEQ, q * 512:(q + 1) * 512]
                V.tensor_copy(dst, ps[0:n, i % 8, :]).then_inc(y_copied, 1)


OUTS = [("y_prompt", (1, SEQ, DM)), ("y_sample", (1, DSEQ, DM)),
        ("a_k_p", (DEPTH, 1, WINDOW, 2, HD)), ("a_v_p", (DEPTH, 1, WINDOW, 2, HD)),
        ("b_k_p", (DEPTH, 1, SEQ, 4, 2, HD)), ("b_v_p", (DEPTH, 1, SEQ, 4, 128)),
        ("c_kv_p", (DEPTH, 1, SEQ, CKVR)), ("c_krope_p", (DEPTH, 1, SEQ, ROPE)),
        ("d_k_p", (DEPTH, 1, SEQ, 8, HD)), ("d_v_p", (DEPTH, 1, SEQ, 8, HD)), ("d_logf_p", (DEPTH, 1, SEQ, 8)),
        ("a_k_s", (DEPTH, 1, WINDOW, 2, HD)), ("a_v_s", (DEPTH, 1, WINDOW, 2, HD)),
        ("b_k_s", (DEPTH, 1, DSEQ, 4, 2, HD)), ("b_v_s", (DEPTH, 1, DSEQ, 4, 128)),
        ("c_kv_s", (DEPTH, 1, DSEQ, CKVR)), ("c_krope_s", (DEPTH, 1, DSEQ, ROPE)),
        ("d_k_s", (DEPTH, 1, DSEQ, 8, HD)), ("d_v_s", (DEPTH, 1, DSEQ, 8, HD)), ("d_logf_s", (DEPTH, 1, DSEQ, 8))]


def constants():
    import math
    import numpy as np
    t = np.zeros((128, T_END), np.float32)
    p = np.arange(128)
    t[:, T_ID:T_ID + 128] = np.eye(128)
    t[:, T_TRI:T_TRI + 128] = p[:, None] <= p[None, :]
    q, k = 128 + p[:, None], np.arange(256)[None, :]
    dist = -np.abs(q - k).astype(np.float32)
    qc, kc = q // CHUNK, k // CHUNK
    t[:, T_NDA:T_NDA + 256] = np.where((kc <= qc) & (kc >= qc - WINDOW // CHUNK), dist, NEG)
    t[:, T_NDB:T_NDB + 256] = np.where(kc <= qc, dist, NEG)
    t[:, T_MC:T_MC + 128] = np.where(p[None, :] // CHUNK <= p[:, None] // CHUNK, 0, NEG)
    t[:, T_MD:T_MD + 128] = np.where(p[None, :] <= p[:, None], 0, NEG)
    t[:, T_NDS:T_NDS + KEYS] = -np.abs(PAST + p[:, None] - np.arange(KEYS)[None, :])
    half = ROPE // 2
    inv = np.float32(10000.0) ** (-np.arange(half, dtype=np.float32) / np.float32(half))
    for tile, first in enumerate((0, 128, PAST)):
        ang = ((first + p).astype(np.float32)[:, None] * inv).astype(np.float32)
        t[:, T_COS + 16 * tile:T_COS + 16 * (tile + 1)] = np.cos(ang)
        t[:, T_SIN + 16 * tile:T_SIN + 16 * (tile + 1)] = np.sin(ang)
    lam = [0.8 - 0.6 * math.exp(-0.3 * li) for li in range(DEPTH)]
    return {"table": t, "lam_init": np.array([[v, 1.0 - v] for v in lam], np.float32)}


def kernel(**inputs):
    import numpy as np
    import concourse.bacc as bacc
    from concourse.bass_utils import run_bass_kernel_spmd

    nc = bacc.Bacc("TRN2", target_bir_lowering=False, num_devices=1)
    arrays, I, O = {}, {}, {}
    for name, a in {**inputs, **constants()}.items():
        a = np.ascontiguousarray(a)
        arrays[f"in_{name}"] = a
        I[name] = nc.dram_tensor(f"in_{name}", a.shape, mybir.dt.from_np(a.dtype), kind="ExternalInput").ap()
    for name, shape in OUTS:
        O[name] = nc.dram_tensor(f"out_{name}", shape, mybir.dt.float32, kind="ExternalOutput").ap()
    build(nc, I, O)
    r = run_bass_kernel_spmd(nc, [arrays], core_ids=[0])
    return tuple(r.results[0][f"out_{name}"] for name, _ in OUTS)
```
